# Optimizing a Trainium2 kernel written in Bass

```python
import jax, jax.numpy as jnp
from jax import lax
import numpy as np
import math

D_MODEL = 1024
BATCH = 1
SEQ = 512
DEPTH = 2

HEAD_DIM = 64
EPS = 1e-6
LRU_WIDTH = D_MODEL // 2
LRU_BLOCKS = 8
LRU_BLOCK = LRU_WIDTH // LRU_BLOCKS
LRU_CONV = 4
LRU_C = 8.0
SB_HEADS = 8
SB_WIDTH = SB_HEADS * HEAD_DIM
Q_BLOCK = 128
N_EVEN_SPLITS = 5
SWA_HEADS = D_MODEL // HEAD_DIM
SWA_KV_HEADS = 4
SWA_GROUP = SWA_HEADS // SWA_KV_HEADS
WINDOW = 128
D_FF = 2816
FFN_CONV = 3
N_EVEN = (DEPTH + 1) // 2
N_ODD = DEPTH // 2


def rms_norm(x, g):
    xf = x.astype(jnp.float32)
    y = xf * lax.rsqrt(jnp.mean(xf * xf, axis=-1, keepdims=True) + EPS)
    return (y * g.astype(jnp.float32)).astype(x.dtype)

def causal_dwconv(x, w, b):
    k_width, ch = w.shape
    y = lax.conv_general_dilated(
        x, w[:, None, :].astype(x.dtype), window_strides=(1,),
        padding=[(k_width - 1, 0)], dimension_numbers=("NWC", "WIO", "NWC"),
        feature_group_count=ch)
    return y + b.astype(x.dtype)

def adaln_params(c, w, b):
    m = jax.nn.silu(c) @ w + b
    return [t[:, None, :] for t in jnp.split(m, 6, axis=-1)]

def rg_lru(x, wa, ba, wx, bx, lam):
    bsz, seq, width = x.shape
    xb = x.reshape(bsz, seq, LRU_BLOCKS, LRU_BLOCK)
    r = jax.nn.sigmoid((jnp.einsum("bsnk,nkj->bsnj", xb, wa).reshape(bsz, seq, width) + ba).astype(jnp.float32))
    i = jax.nn.sigmoid((jnp.einsum("bsnk,nkj->bsnj", xb, wx).reshape(bsz, seq, width) + bx).astype(jnp.float32))
    log_a = -LRU_C * r * jax.nn.softplus(-lam.astype(jnp.float32))
    a = jnp.exp(log_a)
    u = jnp.sqrt(-jnp.expm1(2.0 * log_a)) * (i * x.astype(jnp.float32))

    def combine(e1, e2):
        a1, b1 = e1
        a2, b2 = e2
        return a1 * a2, a2 * b1 + b2

    _, h = lax.associative_scan(combine, (a, u), axis=1)
    return h.astype(x.dtype)

def stick_breaking(q, k, v):
    bsz, seq, heads, dh = q.shape
    nb = seq // Q_BLOCK
    scale = 1.0 / np.sqrt(dh)
    qb = q.reshape(bsz, nb, Q_BLOCK, heads, dh).transpose(1, 0, 3, 2, 4)
    kh = k.transpose(0, 2, 1, 3)
    vh = v.transpose(0, 2, 1, 3)
    kpos = jnp.arange(seq)

    def block(args):
        qi, blk = args
        z = jnp.einsum("bhqd,bhkd->bhqk", qi, kh).astype(jnp.float32) * scale
        qpos = blk * Q_BLOCK + jnp.arange(Q_BLOCK)
        mask = kpos[None, :] < qpos[:, None]
        sp = jnp.where(mask, jax.nn.softplus(z), 0.0)
        rev = lax.cumsum(sp, axis=3, reverse=True)
        w = jnp.exp(jnp.where(mask, z - rev, -jnp.inf))
        return jnp.einsum("bhqk,bhkd->bhqd", w.astype(v.dtype), vh)

    out = lax.map(block, (qb, jnp.arange(nb)))
    return out.transpose(1, 0, 3, 2, 4).reshape(bsz, seq, heads * dh)

def swa_sinks(q, k, v, sinks):
    bsz, seq, _, dh = q.shape
    nb = seq // WINDOW
    scale = 1.0 / np.sqrt(dh)
    qb = q.reshape(bsz, nb, WINDOW, SWA_KV_HEADS, SWA_GROUP, dh)

    def banded(t):
        tb = t.reshape(bsz, nb, WINDOW, SWA_KV_HEADS, dh)
        prev = jnp.concatenate([jnp.zeros_like(tb[:, :1]), tb[:, :-1]], axis=1)
        return jnp.concatenate([prev, tb], axis=2)

    kk, vv = banded(k), banded(v)
    s = jnp.einsum("bnqkgd,bnjkd->bnkgqj", qb, kk).astype(jnp.float32) * scale
    i = jnp.arange(WINDOW)[:, None]
    j = jnp.arange(2 * WINDOW)[None, :]
    band = (j > i) & (j <= i + WINDOW)
    blk = jnp.arange(nb)[:, None, None]
    mask = band[None] & ((j >= WINDOW)[None] | (blk > 0))
    s = jnp.where(mask[None, :, None, None], s, -jnp.inf)
    sink = sinks.astype(jnp.float32).reshape(SWA_KV_HEADS, SWA_GROUP)[None, None, :, :, None, None]
    m = jnp.maximum(jnp.max(s, axis=-1, keepdims=True), sink)
    p = jnp.exp(s - m)
    p = p / (jnp.sum(p, axis=-1, keepdims=True) + jnp.exp(sink - m))
    out = jnp.einsum("bnkgqj,bnjkd->bnqkgd", p.astype(v.dtype), vv)
    return out.reshape(bsz, seq, SWA_HEADS * dh)

def conv_ffn(h, w_gate, w_up, conv_w, conv_b, w_down):
    a = causal_dwconv(h @ w_gate, conv_w, conv_b)
    return (jax.nn.silu(a) * (h @ w_up)) @ w_down

def first_inputs(seed: int = 0) -> dict:
    key = jax.random.key(seed)
    ks = iter(jax.random.split(key, 40))

    def nrm(shape, scale):
        return jax.random.normal(next(ks), shape, jnp.float32) * scale

    d = D_MODEL
    u = jax.random.uniform(next(ks), (N_EVEN, LRU_WIDTH), jnp.float32, minval=0.9, maxval=0.999)
    a0 = u ** (1.0 / LRU_C)
    lam = jnp.log(a0) - jnp.log1p(-a0)
    return {
        "x": nrm((BATCH, SEQ, d), 1.0),
        "c": nrm((BATCH, d), 1.0),
        "ada_w": nrm((DEPTH, d, 6 * d), 0.5 * d ** -0.5),
        "ada_b": nrm((DEPTH, 6 * d), 0.02),
        "norm_mix_g": 1.0 + nrm((DEPTH, d), 0.02),
        "norm_ffn_g": 1.0 + nrm((DEPTH, d), 0.02),
        "ev_w_in": nrm((N_EVEN, d, N_EVEN_SPLITS * LRU_WIDTH), d ** -0.5),
        "ev_conv_w": nrm((N_EVEN, LRU_CONV, LRU_WIDTH), LRU_CONV ** -0.5),
        "ev_conv_b": nrm((N_EVEN, LRU_WIDTH), 0.02),
        "ev_wa": nrm((N_EVEN, LRU_BLOCKS, LRU_BLOCK, LRU_BLOCK), LRU_BLOCK ** -0.5),
        "ev_ba": nrm((N_EVEN, LRU_WIDTH), 0.02),
        "ev_wx": nrm((N_EVEN, LRU_BLOCKS, LRU_BLOCK, LRU_BLOCK), LRU_BLOCK ** -0.5),
        "ev_bx": nrm((N_EVEN, LRU_WIDTH), 0.02),
        "ev_lam": lam,
        "ev_qn_g": 1.0 + nrm((N_EVEN, HEAD_DIM), 0.02),
        "ev_kn_g": 1.0 + nrm((N_EVEN, HEAD_DIM), 0.02),
        "ev_w_out": nrm((N_EVEN, LRU_WIDTH + SB_WIDTH, d), (LRU_WIDTH + SB_WIDTH) ** -0.5),
        "od_w_in": nrm((N_ODD, d, (SWA_HEADS + 2 * SWA_KV_HEADS) * HEAD_DIM), d ** -0.5),
        "od_qn_g": 1.0 + nrm((N_ODD, HEAD_DIM), 0.02),
        "od_kn_g": 1.0 + nrm((N_ODD, HEAD_DIM), 0.02),
        "od_sinks": nrm((N_ODD, SWA_HEADS), 1.0),
        "od_w_out": nrm((N_ODD, SWA_HEADS * HEAD_DIM, d), (SWA_HEADS * HEAD_DIM) ** -0.5),
        "ffn_w_gate": nrm((DEPTH, d, D_FF), d ** -0.5),
        "ffn_w_up": nrm((DEPTH, d, D_FF), d ** -0.5),
        "ffn_conv_w": nrm((DEPTH, FFN_CONV, D_FF), FFN_CONV ** -0.5),
        "ffn_conv_b": nrm((DEPTH, D_FF), 0.02),
        "ffn_w_down": nrm((DEPTH, D_FF, d), D_FF ** -0.5),
    }

def first_block(x, c, ada_w, ada_b, norm_mix_g, norm_ffn_g,
              ev_w_in, ev_conv_w, ev_conv_b, ev_wa, ev_ba, ev_wx, ev_bx, ev_lam,
              ev_qn_g, ev_kn_g, ev_w_out,
              od_w_in, od_qn_g, od_kn_g, od_sinks, od_w_out,
              ffn_w_gate, ffn_w_up, ffn_conv_w, ffn_conv_b, ffn_w_down):
    bsz, seq, _ = x.shape
    for layer in range(DEPTH):
        sh1, sc1, g1, sh2, sc2, g2 = adaln_params(c, ada_w[layer], ada_b[layer])
        h = rms_norm(x, norm_mix_g[layer]) * (1.0 + sc1) + sh1
        if layer % 2 == 0:
            e = layer // 2
            xr, gr, q, k, v = jnp.split(h @ ev_w_in[e], N_EVEN_SPLITS, axis=-1)
            xr = causal_dwconv(xr, ev_conv_w[e], ev_conv_b[e])
            hr = rg_lru(xr, ev_wa[e], ev_ba[e], ev_wx[e], ev_bx[e], ev_lam[e])
            ya = hr * jax.nn.gelu(gr)
            q = rms_norm(q.reshape(bsz, seq, SB_HEADS, HEAD_DIM), ev_qn_g[e])
            k = rms_norm(k.reshape(bsz, seq, SB_HEADS, HEAD_DIM), ev_kn_g[e])
            v = v.reshape(bsz, seq, SB_HEADS, HEAD_DIM)
            yb = stick_breaking(q, k, v)
            mix = jnp.concatenate([ya, yb], axis=-1) @ ev_w_out[e]
        else:
            o = layer // 2
            p = h @ od_w_in[o]
            q_w = SWA_HEADS * HEAD_DIM
            kv_w = SWA_KV_HEADS * HEAD_DIM
            q = rms_norm(p[..., :q_w].reshape(bsz, seq, SWA_HEADS, HEAD_DIM), od_qn_g[o])
            k = rms_norm(p[..., q_w:q_w + kv_w].reshape(bsz, seq, SWA_KV_HEADS, HEAD_DIM), od_kn_g[o])
            v = p[..., q_w + kv_w:].reshape(bsz, seq, SWA_KV_HEADS, HEAD_DIM)
            mix = swa_sinks(q, k, v, od_sinks[o]) @ od_w_out[o]
        x = x + g1 * mix
        h = rms_norm(x, norm_ffn_g[layer]) * (1.0 + sc2) + sh2
        x = x + g2 * conv_ffn(h, ffn_w_gate[layer], ffn_w_up[layer], ffn_conv_w[layer],
                              ffn_conv_b[layer], ffn_w_down[layer])
    return x


N_A_LAYERS = DEPTH // 2
N_B_LAYERS = DEPTH - N_A_LAYERS
DIFF_HEADS = D_MODEL // (2 * HEAD_DIM)
DIL_GROUPS = ((128, 1), (512, 4), (2048, 16))
N_GROUPS = len(DIL_GROUPS)
DIL_HEADS = D_MODEL // HEAD_DIM
D_FF_2 = 4 * D_MODEL
ROPE_THETA = 10000.0
BLOCK = 128
LAM_STD = 0.1


def rms_norm_2(x, gain):
    xf = x.astype(jnp.float32)
    y = xf * lax.rsqrt(jnp.mean(xf * xf, axis=-1, keepdims=True) + EPS)
    return (y * gain.astype(jnp.float32)).astype(x.dtype)

def rope_tables(seq, dim):
    inv = 1.0 / (ROPE_THETA ** (jnp.arange(0, dim, 2, dtype=jnp.float32) / dim))
    ang = jnp.arange(seq, dtype=jnp.float32)[:, None] * inv[None, :]
    return jnp.cos(ang), jnp.sin(ang)

def apply_rope(x, cos, sin):
    d2 = x.shape[-1] // 2
    x1, x2 = x[..., :d2], x[..., d2:]
    c = cos[None, :, None, :].astype(x.dtype)
    s = sin[None, :, None, :].astype(x.dtype)
    return jnp.concatenate([x1 * c - x2 * s, x2 * c + x1 * s], axis=-1)

def squared_relu_mlp(x, gain, w_up, w_down):
    h = rms_norm_2(x, gain)
    return jnp.square(jax.nn.relu(h @ w_up)) @ w_down

def diff_attention(h, w_qkv, q_gain, k_gain, lam_q1, lam_k1, lam_q2, lam_k2, sub_gain, lam_init, cos, sin):
    B, S, _ = h.shape
    H, D = DIFF_HEADS, HEAD_DIM
    q, k, v = jnp.split(h @ w_qkv, 3, axis=-1)
    q = apply_rope(rms_norm_2(q.reshape(B, S, 2 * H, D), q_gain), cos, sin).reshape(B, S, H, 2, D)
    k = apply_rope(rms_norm_2(k.reshape(B, S, 2 * H, D), k_gain), cos, sin).reshape(B, S, H, 2, D)
    v = v.reshape(B, S, H, 2 * D)
    f32 = jnp.float32
    lam = (jnp.exp(jnp.sum(lam_q1.astype(f32) * lam_k1.astype(f32)))
           - jnp.exp(jnp.sum(lam_q2.astype(f32) * lam_k2.astype(f32))) + lam_init)
    scale = D ** -0.5
    outs = []
    for i in range(S // BLOCK):
        n_k = (i + 1) * BLOCK
        q_blk = q[:, i * BLOCK:n_k]
        s = jnp.einsum('bqhcd,bkhcd->bhcqk', q_blk, k[:, :n_k]).astype(f32) * scale
        qpos = i * BLOCK + jnp.arange(BLOCK)
        kpos = jnp.arange(n_k)
        s = jnp.where(kpos[None, :] <= qpos[:, None], s, -jnp.inf)
        p = jax.nn.softmax(s, axis=-1)
        a = p[:, :, 0] - lam * p[:, :, 1]
        outs.append(jnp.einsum('bhqk,bkhe->bqhe', a.astype(v.dtype), v[:, :n_k]))
    o = jnp.concatenate(outs, axis=1)
    o = rms_norm_2(o, sub_gain) * (1.0 - lam_init)
    return o.reshape(B, S, H * 2 * D)

def dilated_group_attention(q, k, v, window, dilation):
    B, S, H, D = q.shape
    r = dilation
    L = S // r
    span = window // dilation
    nb = -(-L // BLOCK)
    Lp = nb * BLOCK
    Z = B * r

    def to_sub(a):
        a = a.reshape(B, L, r, H, D).transpose(0, 2, 1, 3, 4).reshape(Z, L, H, D)
        return jnp.pad(a, ((0, 0), (0, Lp - L), (0, 0), (0, 0)))

    def with_prev(a):
        a = jnp.pad(a, ((0, 0), (BLOCK, 0), (0, 0), (0, 0))).reshape(Z, nb + 1, BLOCK, H, D)
        return jnp.concatenate([a[:, :-1], a[:, 1:]], axis=2)

    qb = to_sub(q).reshape(Z, nb, BLOCK, H, D)
    kb = with_prev(to_sub(k))
    vb = with_prev(to_sub(v))
    s = jnp.einsum('znqhd,znkhd->znhqk', qb, kb).astype(jnp.float32) * (D ** -0.5)
    blk = jnp.arange(nb)[:, None, None] * BLOCK
    qi = blk + jnp.arange(BLOCK)[None, :, None]
    kj = blk - BLOCK + jnp.arange(2 * BLOCK)[None, None, :]
    dist = qi - kj
    valid = (dist >= 0) & (dist <= span) & (kj >= 0)
    s = jnp.where(valid[None, :, None], s, -jnp.inf)
    m = jnp.max(s, axis=-1, keepdims=True)
    p = jnp.exp(s - m)
    den = jnp.sum(p, axis=-1)
    o = jnp.einsum('znhqk,znkhd->znqhd', p.astype(vb.dtype), vb).astype(jnp.float32)
    o = o / jnp.transpose(den, (0, 1, 3, 2))[..., None]
    lse = jnp.transpose(m[..., 0] + jnp.log(den), (0, 1, 3, 2))
    o = o.reshape(Z, Lp, H, D)[:, :L].reshape(B, r, L, H, D).transpose(0, 2, 1, 3, 4).reshape(B, S, H, D)
    lse = lse.reshape(Z, Lp, H)[:, :L].reshape(B, r, L, H).transpose(0, 2, 1, 3).reshape(B, S, H)
    return o, lse

def shared_kv(x, kv_norm, kv_w, kv_k_gain, cos, sin):
    B, S, _ = x.shape
    G, H, D = N_GROUPS, DIL_HEADS, HEAD_DIM
    k, v = jnp.split(rms_norm_2(x, kv_norm) @ kv_w, 2, axis=-1)
    k = rms_norm_2(k.reshape(B, S, G, H, D), kv_k_gain[:, None, :])
    k = apply_rope(k.reshape(B, S, G * H, D), cos, sin).reshape(B, S, G, H, D)
    return k, v.reshape(B, S, G, H, D)

def dilated_mixer(x, norm_gain, w_q, q_gain, w_o, k_sh, v_sh, cos, sin):
    B, S, _ = x.shape
    G, H, D = N_GROUPS, DIL_HEADS, HEAD_DIM
    q = rms_norm_2(rms_norm_2(x, norm_gain) @ w_q, jnp.ones((), x.dtype)).reshape(B, S, G, H, D) if False else (rms_norm_2(x, norm_gain) @ w_q).reshape(B, S, G, H, D)
    q = rms_norm_2(q, q_gain[:, None, :])
    q = apply_rope(q.reshape(B, S, G * H, D), cos, sin).reshape(B, S, G, H, D)
    outs, lses = [], []
    for g, (window, dilation) in enumerate(DIL_GROUPS):
        o_g, lse_g = dilated_group_attention(q[:, :, g], k_sh[:, :, g], v_sh[:, :, g], window, dilation)
        outs.append(o_g)
        lses.append(lse_g)
    wts = jax.nn.softmax(jnp.stack(lses, axis=0), axis=0)
    o = jnp.sum(wts[..., None] * jnp.stack(outs, axis=0), axis=0)
    return o.astype(x.dtype).reshape(B, S, H * D) @ w_o

def second_inputs(seed: int = 0) -> dict:
    key = jax.random.key(seed)
    ks = jax.random.split(key, 21)
    f32 = jnp.float32
    nA, nB, G, D = N_A_LAYERS, N_B_LAYERS, N_GROUPS, HEAD_DIM

    def w(k, shape, fan_in):
        return jax.random.normal(k, shape, f32) * (fan_in ** -0.5)

    def gain(k, shape):
        return 1.0 + 0.02 * jax.random.normal(k, shape, f32)

    return {
        'x': jax.random.normal(ks[0], (BATCH, SEQ, D_MODEL), f32),
        'a_norm': gain(ks[1], (nA, D_MODEL)),
        'a_w_qkv': w(ks[2], (nA, D_MODEL, 3 * D_MODEL), D_MODEL),
        'a_q_gain': gain(ks[3], (nA, D)),
        'a_k_gain': gain(ks[4], (nA, D)),
        'a_lam_q1': LAM_STD * jax.random.normal(ks[5], (nA, D), f32),
        'a_lam_k1': LAM_STD * jax.random.normal(ks[6], (nA, D), f32),
        'a_lam_q2': LAM_STD * jax.random.normal(ks[7], (nA, D), f32),
        'a_lam_k2': LAM_STD * jax.random.normal(ks[8], (nA, D), f32),
        'a_sub_gain': gain(ks[9], (nA, 2 * D)),
        'a_w_o': w(ks[10], (nA, D_MODEL, D_MODEL), D_MODEL),
        'kv_norm': gain(ks[11], (D_MODEL,)),
        'kv_w': w(ks[12], (D_MODEL, 2 * G * DIL_HEADS * D), D_MODEL),
        'kv_k_gain': gain(ks[13], (G, D)),
        'b_norm': gain(ks[14], (nB, D_MODEL)),
        'b_w_q': w(ks[15], (nB, D_MODEL, G * DIL_HEADS * D), D_MODEL),
        'b_q_gain': gain(ks[16], (nB, G, D)),
        'b_w_o': w(ks[17], (nB, DIL_HEADS * D, D_MODEL), DIL_HEADS * D),
        'm_norm': gain(ks[18], (DEPTH, D_MODEL)),
        'm_w_up': w(ks[19], (DEPTH, D_MODEL, D_FF_2), D_MODEL),
        'm_w_down': w(ks[20], (DEPTH, D_FF_2, D_MODEL), D_FF_2),
    }

def second_block(x, a_norm, a_w_qkv, a_q_gain, a_k_gain, a_lam_q1, a_lam_k1, a_lam_q2, a_lam_k2,
              a_sub_gain, a_w_o, kv_norm, kv_w, kv_k_gain, b_norm, b_w_q, b_q_gain, b_w_o,
              m_norm, m_w_up, m_w_down):
    S = x.shape[1]
    cos, sin = rope_tables(S, HEAD_DIM)
    k_sh, v_sh = None, None
    for layer in range(DEPTH):
        if layer < N_A_LAYERS:
            lam_init = 0.8 - 0.6 * math.exp(-0.3 * layer)
            h = rms_norm_2(x, a_norm[layer])
            att = diff_attention(h, a_w_qkv[layer], a_q_gain[layer], a_k_gain[layer],
                                 a_lam_q1[layer], a_lam_k1[layer], a_lam_q2[layer], a_lam_k2[layer],
                                 a_sub_gain[layer], lam_init, cos, sin)
            x = x + att @ a_w_o[layer]
        else:
            if layer == N_A_LAYERS:
                k_sh, v_sh = shared_kv(x, kv_norm, kv_w, kv_k_gain, cos, sin)
            bl = layer - N_A_LAYERS
            x = x + dilated_mixer(x, b_norm[bl], b_w_q[bl], b_q_gain[bl], b_w_o[bl], k_sh, v_sh, cos, sin)
        x = x + squared_relu_mlp(x, m_norm[layer], m_w_up[layer], m_w_down[layer])
    return x


def setup_inputs(seed=0):
    out = dict(first_inputs(seed))
    for name, value in second_inputs(seed + 1).items():
        if name != "x":
            out[name + "_2"] = value
    return out


def reference(
    x, c, ada_w, ada_b, norm_mix_g, norm_ffn_g, ev_w_in, ev_conv_w, ev_conv_b, ev_wa, ev_ba,
    ev_wx, ev_bx, ev_lam, ev_qn_g, ev_kn_g, ev_w_out, od_w_in, od_qn_g, od_kn_g, od_sinks,
    od_w_out, ffn_w_gate, ffn_w_up, ffn_conv_w, ffn_conv_b, ffn_w_down, a_norm_2, a_w_qkv_2,
    a_q_gain_2, a_k_gain_2, a_lam_q1_2, a_lam_k1_2, a_lam_q2_2, a_lam_k2_2, a_sub_gain_2,
    a_w_o_2, kv_norm_2, kv_w_2, kv_k_gain_2, b_norm_2, b_w_q_2, b_q_gain_2, b_w_o_2, m_norm_2,
    m_w_up_2, m_w_down_2,
):
    x = first_block(
        x, c, ada_w, ada_b, norm_mix_g, norm_ffn_g, ev_w_in, ev_conv_w, ev_conv_b, ev_wa, ev_ba,
        ev_wx, ev_bx, ev_lam, ev_qn_g, ev_kn_g, ev_w_out, od_w_in, od_qn_g, od_kn_g, od_sinks,
        od_w_out, ffn_w_gate, ffn_w_up, ffn_conv_w, ffn_conv_b, ffn_w_down,
    )
    return second_block(
        x, a_norm_2, a_w_qkv_2, a_q_gain_2, a_k_gain_2, a_lam_q1_2, a_lam_k1_2, a_lam_q2_2,
        a_lam_k2_2, a_sub_gain_2, a_w_o_2, kv_norm_2, kv_w_2, kv_k_gain_2, b_norm_2, b_w_q_2,
        b_q_gain_2, b_w_o_2, m_norm_2, m_w_up_2, m_w_down_2,
    )


_drawn_inputs = setup_inputs


def setup_inputs(seed=0):
    import zlib

    import numpy as np

    out = dict(_drawn_inputs(seed))
    spreads = {}
    factors = {'norm_mix_g': 6.274,
     'norm_ffn_g': 5.214,
     'ev_ba': 8.0,
     'ev_bx': 8.0,
     'ev_qn_g': 8.0,
     'ev_kn_g': 8.0,
     'od_qn_g': 8.0,
     'od_kn_g': 8.0,
     'od_sinks': 4.042,
     'ffn_conv_b': 6.882,
     'a_norm_2': 2.862,
     'a_q_gain_2': 5.462,
     'a_k_gain_2': 5.428,
     'a_lam_q1_2': 5.415,
     'a_lam_k1_2': 4.597,
     'a_sub_gain_2': 4.603,
     'kv_norm_2': 8.0,
     'kv_k_gain_2': 8.0,
     'b_norm_2': 8.0,
     'b_q_gain_2': 8.0,
     'm_norm_2': 2.729,
     'a_lam_q2_2': 3.791,
     'a_lam_k2_2': 2.979}
    for name, (base, spread) in spreads.items():
        noise = np.random.default_rng([zlib.crc32(name.encode()), seed]).standard_normal(out[name].shape)
        drawn = base * np.exp(spread * noise) if base else spread * noise
        out[name] = __import__('jax').numpy.asarray(drawn.astype(out[name].dtype))
    for name, factor in factors.items():
        out[name] = (out[name] * factor).astype(out[name].dtype)
    return out
```

```python
from contextlib import ExitStack
import math

import numpy as np

import concourse.bass as bass
from concourse import mybir

F32 = mybir.dt.float32
F32R = mybir.dt.float32r
BF16 = mybir.dt.bfloat16
ALU = mybir.AluOpType
ACT = mybir.ActivationFunctionType
AX = mybir.AxisListType

P = 128
S = 512
D = 1024
DC = D // P
DH = 64
NB = S // P
FF = 2816
FC = FF // P
PARTS = ((0, 8), (8, 8), (16, 6))
FF2 = 4096
LW = 512
LC = LW // P
EPS = 1e-6
NEG = -1e30
LAM_INIT = 0.8 - 0.6 * math.exp(-0.3 * 0)
GROUPS = 3
CR = 16
DIL = (1, 4, 16)

M_PS, M_C1, M_PE, M_C, M_4, M_16, T_C, T_PS, T_PE, T_B, T_S = range(11)
N_MASK = 11


def constants():
    i = np.arange(P)[:, None]
    j = np.arange(P)[None, :]
    d = i - j
    allowed = [
        j > i, d >= 0, j >= i, d >= 0, d % 4 == 0, d % 16 == 0,
        d <= 0, i > j, i >= j,
        (d % 4 == 0) & (d <= 0), i < j,
    ]
    masks = np.stack([np.where(a, 0.0, NEG) for a in allowed], 1).astype(np.float32)
    inv = (1.0 / (np.float32(10000.0) ** (np.arange(0, DH, 2, dtype=np.float32) / np.float32(DH)))).astype(np.float32)
    ang = np.arange(S, dtype=np.float32)[None, :] * inv[:, None]
    cos = np.tile(np.cos(ang), (4, 1)).astype(np.float32)
    sin = np.tile(np.sin(ang), (4, 1)).astype(np.float32)
    heads = (i // DH == j // DH).astype(np.float32)
    rot = np.zeros((P, P), np.float32)
    for m in range(P):
        if m % DH < DH // 2:
            rot[m + DH // 2, m] = -1.0
        else:
            rot[m - DH // 2, m] = 1.0
    square = np.concatenate([
        np.eye(P, dtype=np.float32), np.ones((P, P), np.float32), heads, rot,
        np.where(i >= j, -1.0, 0.0).astype(np.float32), -np.ones((P, P), np.float32),
        cos, sin], 1)
    return {"masks": masks.reshape(P, N_MASK * P), "square": np.ascontiguousarray(square)}


class Params:

    def __init__(self):
        self.rows, self.at = 0, {}

    def add(self, name, n):
        self.at[name] = self.rows
        self.rows += n


def param_table():
    t = Params()
    for name, n in [("ada_b", 96), ("c", 8), ("norm_mix_g", 16), ("ev_ba", 4), ("ev_bx", 4),
                    ("norm_ffn_g", 16), ("a_norm", 8), ("kv_norm", 8), ("b_norm", 8), ("m_norm", 16),
                    ("ev_conv_w", 16), ("ev_conv_b", 4), ("ev_lam", 4), ("a_sub_gain", 1),
                    ("gains", 12), ("pad", 31),
                    ("ffn_conv_w", 132), ("ffn_conv_b", 44)]:
        t.add(name, n)
    return t


PT = param_table()
PT_TILES = -(-PT.rows // P)
GAINS = ["ev_qn_g", "ev_kn_g", "od_qn_g", "od_kn_g", "a_q_gain_2", "a_k_gain_2",
         "kv_k_gain_2", None, None, "b_q_gain_2", None, None]
G_EVQ, G_EVK, G_ODQ, G_ODK, G_AQ, G_AK, G_KV, G_B = 0, 1, 2, 3, 4, 5, 6, 9


class Stage:
    unit = 0
    seen = {}

    def __init__(self, kind, n, kc, weights, rhs, gain=0, dest=0, rope=False, perm=0, gate=None, source="", layer=0, first=0):
        self.kind, self.n, self.kc, self.weights, self.rhs = kind, n, kc, weights, rhs
        self.gain, self.dest, self.rope, self.perm, self.gate = gain, dest, rope, perm, gate
        self.source, self.layer, self.first = source, layer, first
        self.next_kc = None
        self.base = Stage.unit
        Stage.unit += n
        self.kbase = Stage.seen.get(kind, 0)
        Stage.seen[kind] = self.kbase + n
        self.rbase = Stage.seen.get("rope", 0)
        if rope:
            Stage.seen["rope"] = self.rbase + n


def program(nc, a, out):
    Stage.unit, Stage.seen = 0, {}
    ctx = ExitStack()

    def sb(name, shape, dt=F32, where=ctx):
        return where.enter_context(nc.sbuf_tensor(name, shape, dt))

    def sem(name):
        return ctx.enter_context(nc.semaphore(name))

    def past(n):
        return n + CR

    with ctx:
        raw = [sb(f"w_raw{j}", [P, DC * P]) for j in range(2)]
        whi = [sb(f"w_hi{j}", [P, DC * P], F32R) for j in range(2)]
        wlo = [sb(f"w_lo{j}", [P, DC * P], F32R) for j in range(2)]
        xT = sb("xT", [P, DC * S])
        yhi = sb("y_hi", [P, DC * S], F32R)
        ylo = sb("y_lo", [P, DC * S], F32R)
        sq9 = sb("squares", [P, 6 * P + 2 * S])
        ident, ones, blk64, rotm, ntri, nones = (sq9[:, k * P:(k + 1) * P] for k in range(6))
        cosT, sinT = sq9[:, 6 * P:6 * P + S], sq9[:, 6 * P + S:6 * P + 2 * S]
        maskb = sb("mask_b", [P, N_MASK * P], BF16)
        identb = sb("ident_b", [P, P], BF16)
        onesr = sb("ones_r", [P, P], F32R)
        PV = sb("params", [P, PT_TILES * P])
        MOD = sb("mods", [P, 96])
        NA = sb("norm_scale", [P, 4 * DC])
        small = sb("small", [P, 64])
        lamv = small[:, 0:1]
        c8 = small[:, 4:8]
        sinkb = sb("sink_b", [P, 16])
        subg = small[:, 8:9]

        def mask(m):
            return maskb[:, m * P:(m + 1) * P]

        def masks_to(end, n):
            return maskb[:, (end - n) * P:end * P]

        def col(name, k=0, n=1):
            at = PT.at[name]
            return PV[:, at + k:at + k + n] if isinstance(k, int) else PV[:, bass.ds(k + at, n)]

        def gain(k):
            return PV[:, PT.at["gains"] + k:PT.at["gains"] + k + 1]

        u1 = ExitStack()
        with u1:
            hhi = sb("h_hi", [P, DC * S], F32R, u1)
            hlo = sb("h_lo", [P, DC * S], F32R, u1)
        u2 = ExitStack()
        with u2:
            qs_hi = sb("q_hi", [P, GROUPS * S], F32R, u2)
            qs_lo = sb("q_lo", [P, GROUPS * S], F32R, u2)
            ks_hi = sb("k_hi", [P, GROUPS * S], F32R, u2)
            ks_lo = sb("k_lo", [P, GROUPS * S], F32R, u2)
            diag = sb("diag", [P, S], F32R, u2)
            ytile = sb("y_tile", [P, S], F32, u2)
            extra = sb("extra", [P, S], F32, u2)
            m2 = sb("m2", [P, 8], F32, u2)
            negm = sb("negm", [P, 4], F32, u2)
        sb("h_space", [P, 2 * DC * S])
        TMP = sb("tmp", [P, 8 * S])
        tmp = [TMP[:, j * S:(j + 1) * S] for j in range(8)]
        pad = sb("pad", [P, S + 3])
        z1 = ExitStack()
        with z1:
            Z = sb("Z", [P, 36 * S], F32, z1)
        z2 = ExitStack()
        with z2:
            mhi = sb("mid_hi", [P, DC * S], F32R, z2)
            mlo = sb("mid_lo", [P, DC * S], F32R, z2)
        sb("z_space", [P, 36 * S])

        PS = ctx.enter_context(nc.psum_tensor("banks", [P, 8 * S], F32))
        bank = [PS[:, j * S:(j + 1) * S] for j in range(8)]
        G = bank[0:2]

        def zt(k, n=1):
            return Z[:, k * S:(k + n) * S] if isinstance(k, int) else Z[:, bass.ds(k * S, n * S)]

        def ch(t, k, w=S):
            return t[:, k * w:(k + 1) * w] if isinstance(k, int) else t[:, bass.ds(k * w, w)]

        w_raw = [sem("w_raw0"), sem("w_raw1")]
        s_whi, s_wlo = sem("w_hi_ready"), sem("w_lo_ready")
        gemm = sem("gemm_done")
        evac = [sem("evac0"), sem("evac1")]
        bar_pe, bar_act, bar_dve = sem("bar_pe"), sem("bar_act"), sem("bar_dve")
        s_const, s_par, s_x, s_ini, s_out = (sem(n) for n in ("consts", "par", "x_in", "ini", "out_done"))
        s_pt, s_ptc, s_zero = sem("par_t"), sem("par_c"), sem("zeroed")
        s_adaw = [sem(f"ada_w{j}") for j in range(4)]
        s_ada = sem("ada_done")
        s_xt, s_xc = sem("x_t"), sem("x_c")
        n_sq, n_ss, n_ln, n_rstd, n_t, n_hi, n_lo = (sem("n_" + n) for n in ("sq", "ss", "ln", "rstd", "t", "hi", "lo"))
        h_sq, h_ss, h_ln, h_rstd, h_qn, h_rot, h_a, h_b, h_out = (
            sem("h_" + n) for n in ("sq", "ss", "ln", "rstd", "qn", "rot", "a", "b", "out"))
        v_tp, v_out = sem("v_tp"), sem("v_out")
        cv = sem("conv_step")
        f_cv, f_silu, f_hi, f_lo = (sem("f_" + n) for n in ("conv", "silu", "hi", "lo"))
        r_r, r_hi, r_lo = (sem("r_" + n) for n in ("relu", "hi", "lo"))
        l_g, l_a, l_d, l_y = sem("l_gate"), sem("l_act"), sem("l_dve"), sem("l_yhi")
        dv, av = sem("dve_chain"), sem("act_chain")

        W = {n: a[n] for n in a}

        def cols_of(w, k0, kc, first, per):
            def view(i):
                n0 = first + per * i
                c = w[k0:k0 + kc * P, n0:n0 + P] if isinstance(n0, int) else w[k0:k0 + kc * P, bass.ds(n0, P)]
                return c.rearrange("(c p) n -> p c n", p=P)
            return view

        steps = []

        def gemm_stage(kind, n, kc, w, rhs, k0=0, first=0, gain=0, dest=0, rope=False, perm=0, gate=None, source=""):
            st = Stage(kind, n, kc, [cols_of(w, k0, kc, first, 2 * P), cols_of(w, k0, kc, first + P, 2 * P)], rhs,
                       gain=gain, dest=dest, rope=rope, perm=perm, gate=gate, source=source)
            steps.append(("gemm", st))

        norms = [0]

        def norm_step(scale, shift):
            steps.append(("bar", None))
            steps.append(("norm", (norms[0], scale, shift)))
            norms[0] += 1

        def ffn(layer):
            norm_step(lambda c: NA[:, (2 * layer + 1) * DC + c:(2 * layer + 1) * DC + c + 1],
                      lambda c: MOD[:, layer * 48 + 24 + c:layer * 48 + 25 + c])
            wg, wu, wd = (a[n][layer] for n in ("ffn_w_gate", "ffn_w_up", "ffn_w_down"))
            for c0, n in PARTS:
                st = Stage("ffn", 2 * n, DC, [cols_of(wg, 0, DC, c0 * P, P), cols_of(wu, 0, DC, c0 * P, P)],
                           "h", layer=layer, first=c0)
                steps.append(("gemm", st))
                gemm_stage("down", DC, n, wd, "mid", k0=c0 * P, gate=layer * 48 + 40, source="f")

        def mlp(layer):
            norm_step(lambda c: col("m_norm", layer * DC + c), None)
            for part in range(FF2 // D):
                gemm_stage("relu", DC, DC, a["m_w_up_2"][layer], "h", first=part * D)
                gemm_stage("down", DC, DC, a["m_w_down_2"][layer], "mid", k0=part * D, gate=None, source="r")

        norm_step(lambda c: NA[:, c:c + 1], lambda c: MOD[:, c:c + 1])
        ev = a["ev_w_in"][0]
        gemm_stage("conv", 4, DC, ev, "h", first=0)
        gemm_stage("gelu", 4, DC, ev, "h", first=LW)
        steps.append(("bar", None))
        steps.append(("lru", None))
        steps.append(("bar", None))
        gemm_stage("head", 4, DC, ev, "h", first=2 * LW, gain=G_EVQ, dest=24, rope=False)
        gemm_stage("head", 4, DC, ev, "h", first=3 * LW, gain=G_EVK, dest=28, rope=False)
        gemm_stage("v", 4, DC, ev, "h", first=4 * LW, dest=32, perm=0)
        steps += [("bar", None), ("stick", None), ("bar", None)]
        gemm_stage("down", 8, DC, a["ev_w_out"][0], "y", gate=16)
        ffn(0)
        norm_step(lambda c: NA[:, 2 * DC + c:2 * DC + c + 1], lambda c: MOD[:, 48 + c:49 + c])
        od = a["od_w_in"][0]
        gemm_stage("head", 8, DC, od, "h", first=0, gain=G_ODQ, dest=0, rope=False)
        gemm_stage("head", 2, DC, od, "h", first=D, gain=G_ODK, dest=8, rope=False)
        gemm_stage("v", 2, DC, od, "h", first=D + 256, dest=10, perm=0)
        steps += [("bar", None), ("attn", dict(mode="swa", base=0)), ("bar", None)]
        gemm_stage("down", 8, DC, a["od_w_out"][0], "y", gate=48 + 16)
        ffn(1)
        norm_step(lambda c: col("a_norm", c), None)
        qkv = a["a_w_qkv_2"][0]
        gemm_stage("head", 8, DC, qkv, "h", first=0, gain=G_AQ, dest=0, rope=True)
        gemm_stage("head", 8, DC, qkv, "h", first=D, gain=G_AK, dest=8, rope=True)
        gemm_stage("v", 8, DC, qkv, "h", first=2 * D, dest=16, perm=0)
        steps += [("bar", None), ("attn", dict(mode="diff", base=0)), ("bar", None)]
        gemm_stage("down", 8, DC, a["a_w_o_2"][0], "y", gate=None)
        mlp(0)
        for half in range(2):
            norm_step(lambda c: col("kv_norm", c), None)
            for g in range(GROUPS):
                gemm_stage("head", 4, DC, a["kv_w_2"], "h", first=g * D + half * 512, gain=G_KV + g, dest=12 + 4 * g, rope=True)
            for g in range(GROUPS):
                gemm_stage("v", 4, DC, a["kv_w_2"], "h", first=3 * D + g * D + half * 512, dest=24 + 4 * g, perm=g)
            norm_step(lambda c: col("b_norm", c), None)
            for g in range(GROUPS):
                gemm_stage("head", 4, DC, a["b_w_q_2"][0], "h", first=g * D + half * 512, gain=G_B + g, dest=4 * g, rope=True)
            steps += [("bar", None), ("attn", dict(mode="dil", base=4 * half))]
        steps.append(("bar", None))
        gemm_stage("down", 8, DC, a["b_w_o_2"][0], "y", gate=None)
        mlp(1)
        steps.append(("bar", None))

        stages = [st for k, st in steps if k == "gemm"]
        for s0, s1 in zip(stages, stages[1:] + [None]):
            s0.next_kc = s1.kc if s1 else None
            assert s0.base % 2 == 0

        at = {}
        for mode in ("swa", "diff", "dil"):
            at[mode] = {e: sem(f"{mode}_{e}") for e in
                        ("qhi", "qlo", "v", "mx", "red", "negm", "diag", "st", "p", "pv", "rd", "y", "yhi", "ylo", "e", "es", "nrm", "nss", "nl", "nr", "yt")}
        stk = {e: sem(f"stick_{e}") for e in ("hi", "lo", "v", "z", "ab", "ex", "ln", "sp", "rev", "w", "pv", "yhi", "ylo")}

        def par_rows():
            src = {"c": a["c"], "a_sub_gain": a["a_sub_gain_2"], "ev_conv_w": a["ev_conv_w"][0].rearrange("j n -> (j n)"),
                   "ffn_conv_w": a["ffn_conv_w"].rearrange("l j n -> (l j n)")}
            for name in PT.at:
                if name in ("gains", "pad"):
                    continue
                v = src.get(name)
                if v is None:
                    v = a[name] if name in a else a[name + "_2"]
                if len(v.shape) == 2:
                    v = v.rearrange("l n -> (l n)")
                v = v.rearrange("(r n) -> r n", n=P)
                r0, n, done = PT.at[name], v.shape[0], 0
                while done < n:
                    t, o = divmod(r0 + done, P)
                    m = min(n - done, P - o)
                    yield tmp[t][o:o + m, 0:P], v[done:done + m, :]
                    done += m
            for k, name in enumerate(GAINS):
                if name is None:
                    continue
                v = a[name][0] if len(a[name].shape) == 3 else a[name]
                t, o = divmod(PT.at["gains"] + k, P)
                for s in range(2):
                    yield tmp[t][o:o + v.shape[0], DH * s:DH * (s + 1)], v
            for k, (q, kk) in enumerate((("a_lam_q1_2", "a_lam_k1_2"), ("a_lam_q2_2", "a_lam_k2_2"))):
                yield tmp[4 + k][:, 0:DH], a[q].to_broadcast([P, DH])
                yield tmp[4 + k][:, DH:2 * DH], a[kk].to_broadcast([P, DH])
            yield sinkb[:, :], a["od_sinks"].to_broadcast([P, 16])

        par_loads = list(par_rows())
        N_PAR = len(par_loads)
        dv2, s_kdup, s_vd = sem("dve_start"), sem("k_dup"), sem("v_rows")
        eps = small[:, 60:61]

        def starts(eng, owned):
            for s in owned:
                eng.sem_inc(s, CR)

        def quads(mode, g):
            if mode == "diff":
                return [[(0, S - kt * P, kt, kt * P, [(0, T_C)])] for kt in range(NB)]
            if g == 0:
                prev = T_PS if mode == "swa" else T_PE
                r = [(0, 256, 0, 0, [(0, T_C), (P, prev)]), (256, 256, 1, P, [(0, T_C), (P, prev)])]
                r2 = [(0, 256, 2, 2 * P, [(0, T_C), (P, prev)]), (256, P, 3, 3 * P, [(0, T_C)])]
                return [r, r2]
            m = T_C if g == 1 else T_B
            return [[(c * P, P, c, c, [(0, m)]) for c in range(NB)]]

        def perm(g, c, n, first):
            def view(t, off):
                if g == 0:
                    return t[:, off + first:off + first + n]
                v = t[:, off:off + S]
                return v.rearrange("p (l s) -> p s l", s=4)[:, c, :]
            return view

        def quad_list(mode):
            gs = range(GROUPS) if mode == "dil" else [0]
            return [(g, q) for g in gs for q in quads(mode, g)]

        def layout(mode):
            if mode == "swa":
                return dict(loops=4, sub=2, ng=1, q=lambda j, s, g: 2 * j + s, k=None, nq=2)
            if mode == "diff":
                return dict(loops=8, sub=1, ng=1, q=lambda j, s, g: j, k=lambda j, s, g: 8 + j, nq=4)
            return dict(loops=4, sub=1, ng=3, q=lambda j, s, g: 4 * g + j, k=lambda j, s, g: 12 + 4 * g + j, nq=4)

        KDUP = 14
        ST = bank[3:5]

        VW = 3 * DH

        def room(mode):
            if mode == "dil":
                return TMP[:, 0:12 * VW], [TMP[:, 12 * VW + j * S:12 * VW + (j + 1) * S] for j in range(2)], TMP[:, 12 * VW + 2 * S:12 * VW + 3 * S]
            return Z[:, 24 * S:24 * S + 4 * VW], [zt(26 + j) for j in range(4)], zt(30)

        block = ctx.enter_context(nc.Block())

        @block.sync
        def _(sp):
            sp.dma_start(sq9[:, :], a["square"]).then_inc(s_const, 16)
            sp.dma_start(Z[:, 0:N_MASK * P], a["masks"]).then_inc(s_const, 16)
            sp.wait_ge(s_zero, 1)
            for w, name in enumerate(("ev_wa", "ev_wx")):
                for b in range(2):
                    tiles = Z[64 * b:64 * b + 64, 32 * S:34 * S].rearrange("p (t w n) -> p t w n", w=2, n=P)
                    sp.dma_start(tiles[:, :, w, 64 * b:64 * b + 64],
                                 a[name][0].rearrange("(t b) k j -> b k t j", b=2)[b]).then_inc(s_const, 16)
            sp.dma_start(zt(6, 8).rearrange("p (b d) -> p b d", b=NB),
                         a["x"][0].rearrange("(b p) d -> p b d", p=P)).then_inc(s_x, 16)
            slab = DC * 2 * P
            for n in range(48):
                if n >= 4:
                    sp.wait_ge(s_ada, n - 3)
                layer, c0 = divmod(n * 2 * P, 6 * D)
                sp.dma_start(Z[:, 16 * S + (n % 4) * slab:16 * S + (n % 4 + 1) * slab].rearrange("p (c n) -> p c n", c=DC),
                             a["ada_w"][layer][:, c0:c0 + 2 * P].rearrange("(c p) n -> p c n", p=P)).then_inc(s_adaw[n % 4], 16)

            def load(st, i, j):
                u = st.base + j + 2 * i
                half = st.base // 2 + i
                sp.wait_ge(s_wlo, past(u - 1))
                sp.dma_start(raw[j][:, 0:st.kc * P].rearrange("p (c n) -> p c n", n=P), st.weights[j](i)).then_inc(w_raw[j], 16)

            for st in stages:
                lo = 0
                if st.base == 0:
                    load(st, 0, 0)
                    load(st, 0, 1)
                    lo = 1
                if st.n // 2 - lo <= 1:
                    for i in range(lo, st.n // 2):
                        load(st, i, 0)
                        load(st, i, 1)
                else:
                    with sp.Fori(lo, st.n // 2) as i:
                        load(st, i, 0)
                        load(st, i, 1)
            for t in range(NB):
                for hh in range(2):
                    sp.wait_ge(s_xc, DC + 2 * t + hh + 1)
                    sp.dma_start(out[0, t * P:(t + 1) * P, hh * S:(hh + 1) * S], zt(2 * t + hh)).then_inc(s_out, 16)
            sp.wait_ge(s_out, 16 * 2 * NB)

        @block.gpsimd
        def _(pool):
            starts(pool, [s_wlo])

            def split(st, i, j):
                u = st.base + j + 2 * i
                pool.wait_ge(s_whi, past(u + 1))
                n = st.kc * P
                pool.tensor_tensor(wlo[j][:, 0:n], raw[j][:, 0:n], whi[j][:, 0:n], ALU.subtract).then_inc(s_wlo, 1)

            for st in stages:
                if st.n <= 2:
                    split(st, 0, 0)
                    split(st, 0, 1)
                else:
                    with pool.Fori(0, st.n // 2) as i:
                        split(st, i, 0)
                        split(st, i, 1)

        def run_units(eng, st, do):
            b, n = st.base, st.n

            def unit(i, par):
                return 2 * i + par, par, 2 * i + (b + par), i + b // 2

            do(unit(0, 0), None)
            if n > 4:
                with eng.Fori(0, (n - 2) // 2) as i:
                    do(unit(i, 1), unit(i, 0))
                    do(unit(i + 1, 0), unit(i, 1))
            elif n == 4:
                do(unit(0, 1), unit(0, 0))
                do(unit(1, 0), unit(0, 1))
            do(unit(n // 2 - 1, 1), unit(n // 2 - 1, 0))

        @block.tensor
        def _(pe):
            starts(pe, [at[m][e] for m in at for e in ("mx", "st", "pv", "e", "nss")] + [stk[e] for e in ("z", "rev", "pv")]
                   + [h_ss, h_rot, v_tp, n_ss, gemm])
            nbar = [0]
            pending = [None]

            def bar():
                flush()
                nbar[0] += 1
                pe.drain().then_inc(bar_pe, 1)
                pe.wait_ge(bar_act, nbar[0])
                pe.wait_ge(bar_dve, nbar[0])

            def flush():
                if pending[0]:
                    pending[0]("a")
                    pending[0]("b")
                pending[0] = None

            def post(st, l, par, u, half):
                k = st.kbase + l
                kr = st.rbase + l

                def head(part):
                    if part == "a":
                        pe.wait_ge(h_sq, past(k + 1))
                        pe.wait_ge(h_ln, past(k))
                        pe.matmul(bank[2], blk64, tmp[0], start=True, stop=True).then_inc(h_ss, 1)
                    elif st.rope:
                        pe.wait_ge(h_qn, past(k + 1))
                        pe.wait_ge(h_out, past(kr))
                        pe.matmul(bank[3], rotm, tmp[2], start=True, stop=True).then_inc(h_rot, 1)

                def vpost(part):
                    if part == "a":
                        pe.wait_ge(evac[par], past(half + 1))
                        pe.wait_ge(v_out, past(k))
                        for c in range(NB):
                            view = perm(st.perm, c, P, c * P)(tmp[4], 0)
                            mm = pe.transpose(bank[4][:, c * P:(c + 1) * P], view, ident)
                        mm.then_inc(v_tp, 1)

                return {"head": head, "v": vpost}.get(st.kind, lambda part: None)

            def gemm_units(st):
                hi, lo = {"h": (hhi, hlo), "y": (yhi, ylo), "mid": (mhi, mlo)}[st.rhs]
                def do(this, before):
                    l, par, u, half = this
                    follow = post(st, *before) if before else pending[0]
                    g = G[par]
                    first = isinstance(l, int) and l == 0
                    pe.wait_ge(evac[par], past(half))
                    pe.wait_ge(s_whi, past(u + 1))
                    for k in range(st.kc):
                        ready(st, first, "hi", k)
                        pe.matmul(g, whi[par][:, k * P:(k + 1) * P], hi[:, k * S:(k + 1) * S], start=(k == 0), stop=False)
                    if follow:
                        follow("a")
                    for k in range(st.kc):
                        ready(st, first, "lo", k)
                        pe.matmul(g, whi[par][:, k * P:(k + 1) * P], lo[:, k * S:(k + 1) * S], start=False, stop=False)
                    pe.wait_ge(s_wlo, past(u + 1))
                    for k in range(st.kc):
                        mm = pe.matmul(g, wlo[par][:, k * P:(k + 1) * P], hi[:, k * S:(k + 1) * S], start=False, stop=(k == st.kc - 1))
                    mm.then_inc(gemm, 1)
                    if follow:
                        follow("b")
                    if isinstance(l, int) and l == st.n - 1:
                        pending[0] = post(st, *this)

                run_units(pe, st, do)

            def ready(st, first, part, k):
                if not first:
                    return
                high = part == "hi"
                if st.rhs == "h":
                    pe.wait_ge(n_hi if high else n_lo, past((norm_seen[0] - 1) * DC + k + 1))
                elif st.source == "f":
                    pe.wait_ge(f_hi if high else f_lo, past(mid_base["f"] + k + 1))
                elif st.source == "r":
                    pe.wait_ge(r_hi if high else r_lo, past(mid_base["r"] + k + 1))

            norm_seen = [0]
            mid_base = {"f": 0, "r": 0}

            def norm(ni, scale, shift):
                norm_seen[0] = ni + 1
                for c in range(DC):
                    pe.wait_ge(n_sq, past(DC * ni + c + 1))
                    pe.matmul(bank[2], ones, tmp[c % 2], start=(c == 0), stop=(c == DC - 1)).then_inc(n_ss, 1)

            pe.wait_ge(s_const, 96)
            pe.wait_ge(s_par, 16 * N_PAR)
            for t in range(PT_TILES):
                pe.transpose(bank[t][:, 0:P], tmp[t][:, 0:P], ident).then_inc(s_pt, 1)
            pe.wait_ge(s_x, 16)
            for c in range(DC):
                if c >= 2:
                    pe.wait_ge(s_xc, c - 1)
                for b in range(NB):
                    mm = pe.transpose(bank[5 + c % 2][:, b * P:(b + 1) * P], Z[:, 6 * S + b * D + c * P:6 * S + b * D + (c + 1) * P], ident)
                mm.then_inc(s_xt, 1)
            pe.wait_ge(s_ini, 1)
            for n in range(48):
                pe.wait_ge(s_adaw[n % 4], 16 * (n // 4 + 1))
                base = 16 * S + (n % 4) * DC * 2 * P
                for j in range(2):
                    for k in range(DC):
                        mm = pe.matmul(bank[7][:, 2 * n + j:2 * n + j + 1], Z[:, base + k * 256 + j * P:base + k * 256 + (j + 1) * P],
                                       small[:, 16 + k:17 + k], start=(k == 0), stop=(k == DC - 1))
                mm.then_inc(s_ada, 1)

            def lru():
                for t in range(LC):
                    for w in range(2):
                        wt = Z[:, 32 * S + (2 * t + w) * P:32 * S + (2 * t + w + 1) * P]
                        mm = pe.matmul(bank[4 * w + t], wt, zt(t), start=True, stop=True)
                        mm.then_inc(l_g, 1)

            def stick():
                e = stk
                def head(i, par):
                    h = 2 * i + par
                    r = slice(64 * par, 64 * par + 64)
                    for kt in range(NB - 1, -1, -1):
                        n = S - kt * P
                        z = bank[kt]
                        pe.wait_ge(e["w"], past(4 * h - kt))
                        ks = slice(kt * P, (kt + 1) * P)
                        pe.matmul(z[:, 0:n], ks_hi[r, ks], qs_hi[r, kt * P:S], start=True, stop=False)
                        pe.matmul(z[:, 0:n], ks_hi[r, ks], qs_lo[r, kt * P:S], start=False, stop=False)
                        pe.matmul(z[:, 0:P], identb[:, :], mask(T_S), start=False, stop=False, skip_group_check=True)
                        pe.matmul(z[:, 0:n], ks_lo[r, ks], qs_hi[r, kt * P:S], start=False, stop=True).then_inc(e["z"], 1)
                    for kt in range(NB - 1, -1, -1):
                        n = S - kt * P
                        z = bank[kt]
                        pe.wait_ge(e["sp"], past(4 * h + NB - kt))
                        for k2 in range(NB - 1, kt, -1):
                            o = (k2 - kt) * P
                            pe.matmul(z[:, o:n], nones, zt(16 + k2)[:, 0:S - k2 * P], start=False, stop=False, skip_group_check=True)
                        pe.matmul(z[:, 0:n], ntri, zt(16 + kt)[:, 0:n], start=False, stop=True, skip_group_check=True).then_inc(e["rev"], 1)
                    pe.wait_ge(e["v"], past(i + 1))
                    pe.wait_ge(e["ylo"], past(h))
                    for kt in range(NB - 1, -1, -1):
                        n = S - kt * P
                        pe.wait_ge(e["w"], past(4 * h + NB - kt))
                        mm = pe.matmul(bank[4][r, kt * P:S], zt(8)[:, kt * P + 64 * par:kt * P + 64 * par + 64],
                                       zt(9 + kt)[:, 0:n], start=(kt == NB - 1), stop=(kt == 0), skip_group_check=True)
                    mm.then_inc(e["pv"], 1)

                with pe.Fori(0, 4) as i:
                    pe.wait_ge(e["lo"], past(2 * i + 2))
                    for par in range(2):
                        head(i, par)

            def attn(mode, base):
                e, lay, ql = at[mode], layout(mode), quad_list(mode)
                nq, ng = len(ql), lay["ng"]
                vals, probs, _ = room(mode)

                def head(pp, par):
                    hh = 2 * pp + par
                    r = slice(64 * par, 64 * par + 64)
                    for b in range(NB):
                        pe.wait_ge(e["red"], past(4 * hh + b))
                        bk = bank[0:ng]
                        for g in range(ng):
                            q = qs_hi[r, g * S + b * P:g * S + (b + 1) * P]
                            m = bk[g]
                            if mode == "diff":
                                if b:
                                    pe.matmul(m[:, 0:b * P], q, ks_hi[r, 0:b * P], start=True, stop=True)
                                pe.matmul(m[:, b * P:(b + 1) * P], identb[:, :], mask(M_C), start=True, stop=False)
                                mm = pe.matmul(m[:, b * P:(b + 1) * P], q, ks_hi[r, b * P:(b + 1) * P], start=False, stop=True)
                            elif g == 0:
                                k0 = max(b - 1, 0) * P
                                n = (b + 1) * P - k0
                                pe.matmul(m[:, 0:n], identb[:, :], masks_to((M_C1 if mode == "swa" else M_C) + 1, n // P), start=True, stop=False)
                                mm = pe.matmul(m[:, 0:n], q, ks_hi[r, k0:(b + 1) * P], start=False, stop=True)
                            else:
                                off = mask(M_4 if g == 1 else M_16).rearrange("p (o n) -> p o n", o=1).to_broadcast([P, b + 1, P])
                                pe.matmul(m[:, 0:(b + 1) * P].rearrange("p (o n) -> p o n", o=b + 1), identb[:, :], off, start=True, stop=False)
                                pe.matmul(m[:, b * P:(b + 1) * P], identb[:, :], mask(M_C), start=False, stop=False, skip_group_check=True)
                                mm = pe.matmul(m[:, 0:(b + 1) * P], q, ks_hi[r, g * S:g * S + (b + 1) * P], start=False, stop=True)
                        mm.then_inc(e["mx"], 1)
                    pe.wait_ge(e["diag"], past(hh + 1))
                    if mode == "swa":
                        pe.wait_ge(e["es"], past(hh))
                        pe.matmul(bank[7], onesr[:, :], diag[:, :], start=True, stop=True).then_inc(e["e"], 1)

                    def values(j):
                        g, regions = ql[j]
                        pe.wait_ge(e["p"], past(nq * hh + j + 1))
                        if j == 0:
                            pe.wait_ge(e["v"], past(pp + 1))
                            if mode == "diff":
                                pe.wait_ge(e["y"], past(pp))
                            else:
                                pe.wait_ge(e["y"], past(hh))
                        pb = probs[j % len(probs)]
                        for ri, (c0, n, c, first, _) in enumerate(regions):
                            rhs = pb[:, c0:c0 + n]
                            st_, sp_ = (j == 0 and ri == 0), (j == nq - 1 and ri == len(regions) - 1)
                            if mode == "diff":
                                vt = vals[:, c * P:(c + 1) * P]
                                pe.matmul(bank[5 + par][:, first:first + n], vt, rhs, start=st_, stop=sp_, skip_group_check=True)
                                mm = pe.matmul(bank[(2, 7)[par]][:, first:first + n], ones, rhs, start=st_, stop=sp_, skip_group_check=True)
                            else:
                                vt = vals[:, (g * NB + c) * VW + 64 * par:(g * NB + c) * VW + 64 * par + P]
                                o = perm(g, c, n, first)(bank[5 + par], 0)
                                mm = pe.matmul(o, vt, rhs, start=st_, stop=sp_, skip_group_check=True)
                        mm.then_inc(e["pv"], 1)

                    for j, (g, regions) in enumerate(ql):
                        s = ST[j % 2]
                        pe.wait_ge(e["p"], past(nq * hh + j - 1))
                        for c0, n, c, first, masks in regions:
                            kv = perm(g, c, P, c * P)
                            qv = perm(g, c, n, first)
                            o = s[:, c0:c0 + n]
                            kh, kl = kv(ks_hi[r, :], g * S), kv(ks_lo[r, :], g * S)
                            qh, ql_ = qv(qs_hi[r, :], g * S), qv(qs_lo[r, :], g * S)
                            pe.matmul(o, kh, qh, start=True, stop=False)
                            pe.matmul(o, kh, ql_, start=False, stop=False)
                            pe.matmul(o, kl, qh, start=False, stop=False)
                            for off, m in masks:
                                pe.matmul(s[:, c0 + off:c0 + off + P], identb[:, :], mask(m), start=False, stop=False, skip_group_check=True)
                            mm = pe.matmul(o, onesr[:, :], qv(diag[:, :], 0), start=False, stop=True)
                        mm.then_inc(e["st"], 1)
                        if j >= 1:
                            values(j - 1)
                    values(nq - 1)

                def pair(j, s):
                    pp = base + lay["sub"] * j + s
                    pe.wait_ge(e["qlo"], past((2 * ng) * (pp + 1)))
                    for par in range(2):
                        head(pp, par)
                    if mode == "diff":
                        pe.wait_ge(e["nrm"], past(pp + 1))
                        pe.matmul(bank[1], ones, zt(33), start=True, stop=True).then_inc(e["nss"], 1)

                with pe.Fori(0, lay["loops"]) as j:
                    for s in range(lay["sub"]):
                        pair(j, s)

            for kind, st in steps:
                if kind == "bar":
                    bar()
                elif kind == "norm":
                    norm(*st)
                elif kind == "gemm":
                    gemm_units(st)
                    if st.kind == "down" and st.rhs == "mid":
                        mid_base[st.source] += st.kc
                elif kind == "lru":
                    lru()
                elif kind == "stick":
                    stick()
                else:
                    attn(**st)
            for t in range(NB):
                for hh in range(2):
                    n = 2 * t + hh
                    if n >= 2:
                        pe.wait_ge(s_xc, DC + n - 1)
                    for c in range(4):
                        cc = 4 * hh + c
                        mm = pe.transpose(bank[n % 2][:, c * P:(c + 1) * P], xT[:, cc * S + t * P:cc * S + (t + 1) * P], ident)
                    mm.then_inc(s_xt, 1)


        @block.scalar
        def _(act):
            starts(act, [at[m][e] for m in at for e in ("qhi", "p", "yhi", "es", "nrm", "nl", "nr")]
                   + [stk[e] for e in ("hi", "ab", "ex", "ln", "w", "yhi")]
                   + [h_sq, h_ln, h_rstd, f_silu, f_hi, r_r, r_hi, n_sq, n_ln, n_rstd, n_hi, s_whi])
            nbar, pending = [0], [None]

            def bar():
                if pending[0]:
                    pending[0]()
                pending[0] = None
                nbar[0] += 1
                act.drain().then_inc(bar_act, 1)
                act.wait_ge(bar_pe, nbar[0])
                act.wait_ge(bar_dve, nbar[0])

            act.wait_ge(s_zero, 1)
            for dst, src in par_loads:
                act.dma_start(dst, src).then_inc(s_par, 16)
            act.wait_ge(s_ptc, PT_TILES)
            act.activation(small[:, 16:24], col("c", 0, 8), ACT.Silu).then_inc(s_ini, 1)
            act.activation(small[:, 24:28], col("ev_lam", 0, 4), ACT.Abs).then_inc(av, 1)
            act.wait_ge(av, 1)
            act.activation(small[:, 28:32], small[:, 24:28], ACT.Exp, scale=-1.0).then_inc(av, 1)
            act.wait_ge(dv, 1)
            act.activation(small[:, 36:40], small[:, 32:36], ACT.Ln).then_inc(av, 1)
            act.wait_ge(dv, 3)
            act.activation(small[:, 42:44], small[:, 40:42], ACT.Exp).then_inc(av, 1)

            def high(kc, par, u, half):
                act.wait_ge(w_raw[par], 16 * (half + 1))
                act.wait_ge(gemm, past(u - 1))
                act.activation(whi[par][:, 0:kc * P], raw[par][:, 0:kc * P], ACT.Copy).then_inc(s_whi, 1)

            def post(st, l, par, u, half):
                t = half - st.base // 2
                k = st.kbase + l

                def head():
                    act.wait_ge(gemm, past(u + 1))
                    act.wait_ge(h_ss, past(k))
                    act.activation(tmp[0], G[par], ACT.Square).then_inc(h_sq, 1)
                    act.wait_ge(h_qn, past(k))
                    act.activation(tmp[1], G[par], ACT.Copy).then_inc(evac[par], 1)
                    act.wait_ge(h_ss, past(k + 1))
                    act.wait_ge(h_rstd, past(k))
                    act.activation(tmp[3], bank[2], ACT.Ln, bias=eps, scale=1.0 / DH).then_inc(h_ln, 1)
                    act.wait_ge(h_ln, past(k + 1))
                    act.activation(tmp[6], tmp[3], ACT.Exp, scale=-0.5).then_inc(h_rstd, 1)

                def v():
                    act.wait_ge(gemm, past(u + 1))
                    act.wait_ge(v_tp, past(k))
                    act.activation(tmp[4], G[par], ACT.Copy).then_inc(evac[par], 1)

                def gelu():
                    act.wait_ge(gemm, past(u + 1))
                    act.activation(zt(4 + l), G[par], ACT.Gelu_apprx_tanh).then_inc(evac[par], 1)

                def ffn():
                    kf = st.kbase // 2 + t
                    if par == 0:
                        act.wait_ge(f_cv, past(3 * (kf + 1)))
                        act.wait_ge(evac[1], past(half))
                        act.activation(tmp[1], tmp[0], ACT.Silu).then_inc(f_silu, 1)
                    else:
                        act.wait_ge(evac[1], past(half + 1))
                        act.activation(ch(mhi, t), tmp[2], ACT.Copy).then_inc(f_hi, 1)

                def relu():
                    act.wait_ge(gemm, past(u + 1))
                    act.activation(tmp[0], G[par], ACT.Relu).then_inc(r_r, 1)
                    act.wait_ge(evac[par], past(half + 1))
                    act.activation(ch(mhi, l), tmp[1], ACT.Copy).then_inc(r_hi, 1)

                return {"head": head, "v": v, "gelu": gelu, "ffn": ffn, "relu": relu}.get(st.kind, lambda: None)

            def gemm_units(st):
                def do(this, before):
                    l, par, u, half = this
                    last = isinstance(l, int) and l == st.n - 1
                    kc = st.next_kc if last else st.kc
                    if kc:
                        high(kc, 1 - par, u + 1, half + par)
                    follow = post(st, *before) if before else pending[0]
                    if follow:
                        follow()
                    if last:
                        pending[0] = post(st, *this)

                run_units(act, st, do)

            def norm(ni, scale, shift):
                for c in range(DC):
                    act.wait_ge(n_ss, past(DC * ni + c - 1))
                    act.activation(tmp[c % 2], ch(xT, c), ACT.Square).then_inc(n_sq, 1)
                act.wait_ge(n_ss, past(DC * (ni + 1)))
                act.activation(tmp[2], bank[2], ACT.Ln, bias=eps, scale=1.0 / D).then_inc(n_ln, 1)
                act.wait_ge(n_ln, past(ni + 1))
                act.activation(tmp[3], tmp[2], ACT.Exp, scale=-0.5).then_inc(n_rstd, 1)
                for c in range(DC):
                    act.wait_ge(n_t, past(DC * ni + c + 1))
                    if shift:
                        act.activation(ch(hhi, c), tmp[4 + c % 2], ACT.Identity, bias=shift(c)).then_inc(n_hi, 1)
                    else:
                        act.activation(ch(hhi, c), tmp[4 + c % 2], ACT.Copy).then_inc(n_hi, 1)

            def lru():
                for t in range(LC):
                    act.wait_ge(l_g, 2 * t + 1)
                    act.activation(zt(8 + t), bank[t], ACT.Sigmoid, bias=col("ev_ba", t)).then_inc(l_a, 1)
                    act.wait_ge(l_g, 2 * t + 2)
                    act.activation(zt(12 + t), bank[4 + t], ACT.Sigmoid, bias=col("ev_bx", t)).then_inc(l_a, 1)
                act.wait_ge(l_a, 8)
                for t in range(LC):
                    act.activation(zt(16 + t), zt(8 + t), ACT.Tanh, scale=c8[:, t:t + 1]).then_inc(l_a, 1)
                for t in range(LC):
                    act.activation(zt(8 + t), zt(8 + t), ACT.Exp, scale=c8[:, t:t + 1]).then_inc(l_a, 1)
                act.wait_ge(l_d, 3)
                act.activation(zt(20, 4), zt(20, 4), ACT.Sqrt).then_inc(l_a, 1)
                act.wait_ge(l_d, 10)
                act.activation(yhi[:, 0:LC * S], zt(16, 4), ACT.Copy).then_inc(l_y, 1)

            def stick():
                e = stk

                def pair(i):
                    act.wait_ge(e["z"], past(8 * i))
                    act.activation(qs_hi[:, 0:S], zt(i + 24), ACT.Copy).then_inc(e["hi"], 1)
                    act.activation(ks_hi[:, 0:S], zt(i + 28), ACT.Copy).then_inc(e["hi"], 1)
                    for par in range(2):
                        h = 2 * i + par
                        for kt in range(NB - 1, -1, -1):
                            n = S - kt * P
                            c = 4 * h + NB - kt
                            act.wait_ge(e["z"], past(c))
                            act.wait_ge(e["ex"], past(c - 1))
                            act.activation(zt(13)[:, 0:n], bank[kt][:, 0:n], ACT.Abs).then_inc(e["ab"], 1)
                            act.wait_ge(e["ab"], past(c))
                            act.wait_ge(e["ln"], past(c - 1))
                            act.activation(zt(14)[:, 0:n], zt(13)[:, 0:n], ACT.Exp, scale=-1.0).then_inc(e["ex"], 1)
                            act.wait_ge(e["ex"], past(c))
                            act.wait_ge(e["sp"], past(c - 4))
                            act.activation(zt(20 + kt)[:, 0:n], zt(14)[:, 0:n], ACT.Ln, bias=1.0).then_inc(e["ln"], 1)
                        for kt in range(NB - 1, -1, -1):
                            n = S - kt * P
                            act.wait_ge(e["rev"], past(4 * h + NB - kt))
                            act.wait_ge(e["pv"], past(h))
                            act.activation(zt(9 + kt)[:, 0:n], bank[kt][:, 0:n], ACT.Exp).then_inc(e["w"], 1)
                        r = slice(64 * par, 64 * par + 64)
                        act.wait_ge(e["pv"], past(h + 1))
                        act.activation(yhi[r, bass.ds((i + 4) * S, S)], bank[4][r, :], ACT.Copy).then_inc(e["yhi"], 1)

                with act.Fori(0, 4) as i:
                    pair(i)

            def attn(mode, base):
                e, lay, ql = at[mode], layout(mode), quad_list(mode)
                nq, ng = len(ql), lay["ng"]
                vals, probs, rec = room(mode)

                def pair(j, s):
                    pp = base + lay["sub"] * j + s
                    act.wait_ge(e["st"], past(nq * 2 * pp))
                    for g in range(ng):
                        act.activation(ch(qs_hi, g), zt(lay["q"](j, s, g)), ACT.Copy).then_inc(e["qhi"], 1)
                        src = zt(KDUP + j) if mode == "swa" else zt(lay["k"](j, s, g))
                        act.activation(ch(ks_hi, g), src, ACT.Copy).then_inc(e["qhi"], 1)
                    for par in range(2):
                        hh = 2 * pp + par
                        r = slice(64 * par, 64 * par + 64)
                        if mode == "swa":
                            act.wait_ge(e["e"], past(hh + 1))
                            act.wait_ge(e["rd"], past(2 * hh))
                            act.activation(extra[:, :], bank[7], ACT.Exp, bias=sinkb[:, bass.ds(4 * j + 2 * s + par, 1)]).then_inc(e["es"], 1)
                        for q, (g, regions) in enumerate(ql):
                            n = sum(x[1] for x in regions)
                            act.wait_ge(e["st"], past(nq * hh + q + 1))
                            act.wait_ge(e["pv"], past(nq * hh + q + 1 - len(probs)))
                            act.activation(probs[q % len(probs)][:, 0:n], ST[q % 2][:, 0:n], ACT.Exp).then_inc(e["p"], 1)
                        if mode != "diff":
                            act.wait_ge(e["y"], past(hh + 1))
                            act.activation(yhi[r, bass.ds(pp * S, S)], ytile[r, :], ACT.Copy).then_inc(e["yhi"], 1)
                    if mode == "diff":
                        act.wait_ge(e["y"], past(pp + 1))
                        act.activation(zt(33), zt(32), ACT.Square).then_inc(e["nrm"], 1)
                        act.wait_ge(e["nss"], past(pp + 1))
                        act.wait_ge(e["nr"], past(pp))
                        act.activation(zt(34), bank[1], ACT.Ln, bias=eps, scale=1.0 / P).then_inc(e["nl"], 1)
                        act.wait_ge(e["nl"], past(pp + 1))
                        act.activation(zt(35), zt(34), ACT.Exp, scale=-0.5).then_inc(e["nr"], 1)
                        act.wait_ge(e["yt"], past(pp + 1))
                        act.activation(yhi[:, bass.ds(pp * S, S)], ytile[:, :], ACT.Copy).then_inc(e["yhi"], 1)

                if mode == "swa":
                    act.wait_ge(s_kdup, 1)
                with act.Fori(0, lay["loops"]) as j:
                    for s in range(lay["sub"]):
                        pair(j, s)

            high(DC, 0, 0, 0)
            for kind, st in steps:
                if kind == "bar":
                    bar()
                elif kind == "norm":
                    norm(*st)
                elif kind == "gemm":
                    gemm_units(st)
                elif kind == "lru":
                    lru()
                elif kind == "stick":
                    stick()
                else:
                    attn(**st)

        @block.vector
        def _(dve):
            starts(dve, [at[m][e] for m in at for e in ("qlo", "v", "red", "negm", "diag", "rd", "y", "ylo", "yt")]
                   + [stk[e] for e in ("lo", "v", "sp", "ylo")]
                   + [*evac, n_t, n_lo, h_qn, h_a, h_b, h_out, v_out, cv, f_cv, f_lo, r_lo])
            nbar, pending = [0], [None]

            def bar():
                if pending[0]:
                    pending[0]()
                pending[0] = None
                nbar[0] += 1
                dve.drain().then_inc(bar_dve, 1)
                dve.wait_ge(bar_pe, nbar[0])
                dve.wait_ge(bar_act, nbar[0])

            steps_done = [0]

            def link(ins):
                steps_done[0] += 1
                ins.then_inc(dv2, 1)
                dve.wait_ge(dv2, steps_done[0])

            dve.memset(eps, EPS)
            dve.memset(TMP[:, :], 0.0)
            dve.memset(pad[:, 0:3], 0.0)
            dve.memset(Z[:, 32 * S:34 * S], 0.0).then_inc(s_zero, 1)
            dve.wait_ge(s_const, 96)
            dve.tensor_copy(maskb[:, :], Z[:, 0:N_MASK * P])
            dve.tensor_copy(identb[:, :], ident)
            dve.tensor_copy(onesr[:, :], ones)
            for t in range(PT_TILES):
                dve.wait_ge(s_pt, t + 1)
                dve.tensor_copy(PV[:, t * P:(t + 1) * P], bank[t][:, 0:P]).then_inc(s_ptc, 1)
            dve.wait_ge(s_ptc, PT_TILES)
            for k in (G_EVQ, G_ODQ, G_AQ, G_B, G_B + 1, G_B + 2):
                dve.tensor_scalar(gain(k), gain(k), DH ** -0.5, None, ALU.mult)
            dve.tensor_scalar(subg, col("a_sub_gain"), 1.0 - LAM_INIT, None, ALU.mult)
            dve.wait_ge(av, 2)
            e1, w1, l1 = small[:, 28:32], small[:, 32:36], small[:, 36:40]
            dve.tensor_scalar(w1, e1, 1.0, None, ALU.add).then_inc(dv, 1)
            for k in range(2):
                dve.tensor_tensor_reduce(out=tmp[4 + k][:, 128:192], in0=tmp[4 + k][:, 0:64],
                                         in1=tmp[4 + k][:, 64:128], scale=1.0, scalar=0.0, op0=ALU.mult, op1=ALU.add,
                                         accum_out=small[:, 40 + k:41 + k]).then_inc(dv, 1)
            dve.wait_ge(dv, 1)
            link(dve.scalar_tensor_tensor(small[:, 44:48], w1, -1.0, e1, ALU.add, ALU.subtract))
            link(dve.reciprocal(small[:, 48:52], w1))
            link(dve.tensor_tensor(small[:, 44:48], small[:, 44:48], small[:, 48:52], ALU.mult))
            dve.wait_ge(av, 3)
            link(dve.tensor_tensor(small[:, 44:48], l1, small[:, 44:48], ALU.subtract))
            link(dve.tensor_scalar(small[:, 48:52], col("ev_lam", 0, 4), -1.0, 0.0, ALU.mult, ALU.max))
            link(dve.tensor_tensor(small[:, 44:48], small[:, 44:48], small[:, 48:52], ALU.add))
            link(dve.tensor_scalar(c8, small[:, 44:48], -8.0, None, ALU.mult))
            dve.wait_ge(av, 4)
            link(dve.scalar_tensor_tensor(lamv, small[:, 42:43], LAM_INIT, small[:, 43:44], ALU.add, ALU.subtract))
            for c in range(DC):
                dve.wait_ge(s_xt, c + 1)
                dve.tensor_copy(ch(xT, c), bank[5 + c % 2]).then_inc(s_xc, 1)
            dve.wait_ge(s_ada, 48)
            link(dve.tensor_tensor(MOD[:, :], bank[7][:, 0:96], col("ada_b", 0, 96), ALU.add))
            for layer in range(2):
                for w, name in enumerate(("norm_mix_g", "norm_ffn_g")):
                    o = (2 * layer + w) * DC
                    m = layer * 48 + 8 + 24 * w
                    link(dve.scalar_tensor_tensor(NA[:, o:o + DC], MOD[:, m:m + DC], 1.0, col(name, layer * DC, DC), ALU.add, ALU.mult))

            def post(st, l, par, u, half):
                t = half - st.base // 2
                k = st.kbase + l
                kr = st.rbase + l

                def conv():
                    dve.wait_ge(gemm, past(u + 1))
                    dve.wait_ge(cv, past(4 * l))
                    dve.tensor_copy(pad[:, 3:3 + S], G[par]).then_inc(evac[par], 1)
                    dve.wait_ge(evac[par], past(half + 1))
                    dve.tensor_scalar(zt(l), pad[:, 3:3 + S], col("ev_conv_w", 12 + l), col("ev_conv_b", l), ALU.mult, ALU.add).then_inc(cv, 1)
                    for j in range(1, 4):
                        dve.wait_ge(cv, past(4 * l + j))
                        dve.scalar_tensor_tensor(zt(l), pad[:, 3 - j:3 - j + S], col("ev_conv_w", 4 * (3 - j) + l), zt(l), ALU.mult, ALU.add).then_inc(cv, 1)

                def head():
                    dve.wait_ge(h_rstd, past(k + 1))
                    dve.wait_ge(evac[par], past(half + 1))
                    dest = zt(st.dest + l)
                    if st.rope:
                        dve.wait_ge(h_out, past(kr))
                    dve.scalar_tensor_tensor(tmp[2] if st.rope else dest, tmp[1], gain(st.gain), tmp[6], ALU.mult, ALU.mult).then_inc(h_qn, 1)
                    if st.rope:
                        dve.wait_ge(h_qn, past(k + 1))
                        dve.tensor_tensor(tmp[7], tmp[2], cosT, ALU.mult).then_inc(h_a, 1)
                        dve.wait_ge(h_rot, past(kr + 1))
                        dve.tensor_tensor(tmp[5], bank[3], sinT, ALU.mult).then_inc(h_b, 1)
                        dve.wait_ge(h_a, past(kr + 1))
                        dve.wait_ge(h_b, past(kr + 1))
                        dve.tensor_tensor(dest, tmp[7], tmp[5], ALU.add).then_inc(h_out, 1)

                def v():
                    dve.wait_ge(v_tp, past(k + 1))
                    dve.tensor_scalar(zt(st.dest + l), bank[4], 1.0, None, ALU.mult).then_inc(v_out, 1)

                def ffn():
                    kf = st.kbase // 2 + t
                    if par == 0:
                        o = st.first
                        w = lambda j: col("ffn_conv_w", t + ((st.layer * 3 + j) * FC + o))
                        dve.wait_ge(gemm, past(u + 1))
                        dve.wait_ge(f_cv, past(3 * kf))
                        dve.tensor_copy(pad[:, 3:3 + S], G[0]).then_inc(evac[0], 1)
                        dve.wait_ge(evac[0], past(half + 1))
                        dve.wait_ge(f_silu, past(kf))
                        dve.tensor_scalar(tmp[0], pad[:, 3:3 + S], w(2), col("ffn_conv_b", t + (st.layer * FC + o)), ALU.mult, ALU.add).then_inc(f_cv, 1)
                        for j in range(1, 3):
                            dve.wait_ge(f_cv, past(3 * kf + j))
                            dve.scalar_tensor_tensor(tmp[0], pad[:, 3 - j:3 - j + S], w(2 - j), tmp[0], ALU.mult, ALU.add).then_inc(f_cv, 1)
                    else:
                        dve.wait_ge(gemm, past(u + 1))
                        dve.wait_ge(f_silu, past(kf + 1))
                        dve.wait_ge(f_lo, past(kf))
                        dve.tensor_tensor(tmp[2], G[1], tmp[1], ALU.mult).then_inc(evac[1], 1)
                        dve.wait_ge(f_hi, past(kf + 1))
                        dve.tensor_tensor(ch(mlo, t), tmp[2], ch(mhi, t), ALU.subtract).then_inc(f_lo, 1)

                def relu():
                    dve.wait_ge(r_r, past(k + 1))
                    dve.wait_ge(r_lo, past(k))
                    dve.scalar_tensor_tensor(tmp[1], G[par], 0.0, tmp[0], ALU.max, ALU.mult).then_inc(evac[par], 1)
                    dve.wait_ge(r_hi, past(k + 1))
                    dve.tensor_tensor(ch(mlo, l), tmp[1], ch(mhi, l), ALU.subtract).then_inc(r_lo, 1)

                def down():
                    dve.wait_ge(gemm, past(u + 1))
                    dve.wait_ge(evac[par], past(half))
                    x = ch(xT, l)
                    if st.gate is None:
                        dve.tensor_tensor(x, G[par], x, ALU.add).then_inc(evac[par], 1)
                    else:
                        g = MOD[:, st.gate + l:st.gate + l + 1] if isinstance(l, int) else MOD[:, bass.ds(l + st.gate, 1)]
                        dve.scalar_tensor_tensor(x, G[par], g, x, ALU.mult, ALU.add).then_inc(evac[par], 1)

                return {"conv": conv, "head": head, "v": v, "ffn": ffn, "relu": relu, "down": down}.get(st.kind, lambda: None)

            def gemm_units(st):
                def do(this, before):
                    follow = post(st, *before) if before else pending[0]
                    if follow:
                        follow()
                    if isinstance(this[0], int) and this[0] == st.n - 1:
                        pending[0] = post(st, *this)

                run_units(dve, st, do)

            def norm(ni, scale, shift):
                dve.wait_ge(n_rstd, past(ni + 1))

                def low(c):
                    dve.wait_ge(n_hi, past(DC * ni + c + 1))
                    if shift:
                        dve.scalar_tensor_tensor(ch(hlo, c), tmp[4 + c % 2], shift(c), ch(hhi, c), ALU.add, ALU.subtract).then_inc(n_lo, 1)
                    else:
                        dve.tensor_tensor(ch(hlo, c), tmp[4 + c % 2], ch(hhi, c), ALU.subtract).then_inc(n_lo, 1)

                for c in range(DC):
                    dve.wait_ge(n_lo, past(DC * ni + c - 1))
                    dve.scalar_tensor_tensor(tmp[4 + c % 2], ch(xT, c), scale(c), tmp[3], ALU.mult, ALU.mult).then_inc(n_t, 1)
                    if c:
                        low(c - 1)
                low(DC - 1)

            def lru():
                A, I, T, U = zt(8, 4), zt(12, 4), zt(16, 4), zt(20, 4)
                dve.wait_ge(l_a, 16)
                dve.tensor_scalar(U, T, -1.0, 1.0, ALU.mult, ALU.add).then_inc(l_d, 1)
                dve.wait_ge(l_d, 1)
                dve.reciprocal(U, U).then_inc(l_d, 1)
                dve.wait_ge(l_d, 2)
                dve.scalar_tensor_tensor(U, T, -2.0, U, ALU.mult, ALU.mult).then_inc(l_d, 1)
                dve.tensor_tensor(I, I, zt(0, 4), ALU.mult).then_inc(l_d, 1)
                dve.wait_ge(l_a, 17)
                dve.wait_ge(l_d, 4)
                dve.tensor_tensor(U, U, I, ALU.mult).then_inc(l_d, 1)
                dve.wait_ge(l_d, 5)
                for t in range(LC):
                    dve.tensor_tensor_scan(zt(16 + t), zt(8 + t), zt(20 + t), 0.0, ALU.mult, ALU.add).then_inc(l_d, 1)
                dve.wait_ge(l_d, 9)
                dve.tensor_tensor(T, T, zt(4, 4), ALU.mult).then_inc(l_d, 1)
                dve.wait_ge(l_d, 10)
                dve.wait_ge(l_y, 1)
                dve.tensor_tensor(ylo[:, 0:LC * S], T, yhi[:, 0:LC * S], ALU.subtract)

            def stick():
                e = stk
                with dve.Fori(0, 4) as i:
                    dve.wait_ge(e["hi"], past(2 * i + 1))
                    dve.tensor_tensor(qs_lo[:, 0:S], zt(i + 24), qs_hi[:, 0:S], ALU.subtract).then_inc(e["lo"], 1)
                    dve.wait_ge(e["hi"], past(2 * i + 2))
                    dve.tensor_tensor(ks_lo[:, 0:S], zt(i + 28), ks_hi[:, 0:S], ALU.subtract).then_inc(e["lo"], 1)
                    dve.wait_ge(e["pv"], past(2 * i))
                    dve.tensor_scalar(zt(8), zt(i + 32), 1.0, None, ALU.mult).then_inc(e["v"], 1)
                    for par in range(2):
                        h = 2 * i + par
                        for kt in range(NB - 1, -1, -1):
                            n = S - kt * P
                            dve.wait_ge(e["ln"], past(4 * h + NB - kt))
                            dve.wait_ge(e["rev"], past(4 * h))
                            dve.scalar_tensor_tensor(zt(16 + kt)[:, 0:n], bank[kt][:, 0:n], 0.0, zt(20 + kt)[:, 0:n], ALU.max, ALU.add).then_inc(e["sp"], 1)
                        r = slice(64 * par, 64 * par + 64)
                        dve.wait_ge(e["yhi"], past(h + 1))
                        dve.tensor_tensor(ylo[r, bass.ds((i + 4) * S, S)], bank[4][r, :], yhi[r, bass.ds((i + 4) * S, S)], ALU.subtract).then_inc(e["ylo"], 1)

            def attn(mode, base):
                e, lay, ql = at[mode], layout(mode), quad_list(mode)
                nq, ng = len(ql), lay["ng"]
                vals, probs, rec = room(mode)
                i3 = ident.rearrange("p (o n) -> p o n", o=1).to_broadcast([P, NB, P])

                if mode == "swa":
                    for kv in range(4):
                        src = zt(8 + kv // 2)[64 * (kv % 2):64 * (kv % 2) + 64, :]
                        for o in range(2):
                            dve.tensor_copy(zt(KDUP + kv)[64 * o:64 * o + 64, :], src)
                        dve.tensor_copy(Z[:, 18 * S + kv * 256:18 * S + (kv + 1) * 256].rearrange("p (c d) -> p c d", d=DH),
                                        zt(10 + kv // 2).rearrange("p (c d) -> p c d", d=P)[:, :, 64 * (kv % 2):64 * (kv % 2) + 64]).then_inc(s_vd, 1)
                    dve.wait_ge(s_vd, 4)
                    dve.drain().then_inc(s_kdup, 1)
                    dve.wait_ge(s_kdup, 1)
                if mode != "diff":
                    n = ng * NB
                    v4 = vals.rearrange("p (c h d) -> p c h d", h=3, d=DH)
                    dve.memset(v4[:, :, 1, :], 1.0)

                def values(j, s, pp):
                    dve.wait_ge(e["pv"], past(nq * 2 * pp))
                    if mode == "diff":
                        dve.tensor_scalar(vals[:, 0:S], zt(16 + j), 1.0, None, ALU.mult).then_inc(e["v"], 1)
                        return
                    for g in range(ng):
                        for par in range(2):
                            if mode == "swa":
                                src = Z[:, bass.ds(18 * S + j * 256, 256)].rearrange("p (c d) -> p c d", d=DH)
                            else:
                                src = zt(24 + 4 * g + j).rearrange("p (c d) -> p c d", d=P)[:, :, 64 * par:64 * par + 64]
                            ins = dve.tensor_scalar(v4[:, g * NB:(g + 1) * NB, 2 * par, :], src, 1.0, None, ALU.mult)
                    ins.then_inc(e["v"], 1)

                def pair(j, s):
                    pp = base + lay["sub"] * j + s
                    for g in range(ng):
                        dve.wait_ge(e["qhi"], past(2 * ng * pp + 2 * g + 1))
                        dve.tensor_tensor(ch(qs_lo, g), zt(lay["q"](j, s, g)), ch(qs_hi, g), ALU.subtract).then_inc(e["qlo"], 1)
                        dve.wait_ge(e["qhi"], past(2 * ng * pp + 2 * g + 2))
                        src = zt(KDUP + j) if mode == "swa" else zt(lay["k"](j, s, g))
                        dve.tensor_tensor(ch(ks_lo, g), src, ch(ks_hi, g), ALU.subtract).then_inc(e["qlo"], 1)
                    values(j, s, pp)
                    for par in range(2):
                        hh = 2 * pp + par
                        r = slice(64 * par, 64 * par + 64)
                        o = slice(64 - 64 * par, 128 - 64 * par)
                        dve.wait_ge(e["negm"], past(hh))
                        for b in range(NB):
                            dve.wait_ge(e["mx"], past(4 * hh + b + 1))
                            n = (b + 1) * P if mode == "diff" else (P if b == 0 else 2 * P)
                            if mode == "dil":
                                dve.tensor_reduce(m2[:, 2 * b:2 * b + 1], bank[0][:, 0:n], AX.X, ALU.max)
                                both = PS[:, S:3 * S].rearrange("p (g n) -> p g n", g=2)[:, :, 0:(b + 1) * P]
                                dve.tensor_reduce(m2[:, 2 * b + 1:2 * b + 2], both, AX.XY, ALU.max).then_inc(e["red"], 1)
                            else:
                                dve.tensor_reduce(m2[:, b:b + 1], bank[0][:, 0:n], AX.X, ALU.max).then_inc(e["red"], 1)
                        dve.wait_ge(e["red"], past(4 * hh + 4))
                        dve.wait_ge(e["diag"], past(hh))
                        if mode == "dil":
                            dve.tensor_reduce(negm[:, :], m2[:, 0:8].rearrange("p (b g) -> p b g", g=2), AX.X, ALU.max, negate=True).then_inc(e["negm"], 1)
                        elif mode == "swa":
                            dve.tensor_scalar(negm[:, :], m2[:, 0:4], sinkb[:, bass.ds(4 * j + 2 * s + par, 1)], -1.0, ALU.max, ALU.mult).then_inc(e["negm"], 1)
                        else:
                            dve.tensor_scalar(negm[:, :], m2[:, 0:4], -1.0, None, ALU.mult).then_inc(e["negm"], 1)
                        dve.wait_ge(e["negm"], past(hh + 1))
                        dve.wait_ge(e["st"], past(nq * hh))
                        dve.tensor_tensor(diag[:, :].rearrange("p (b n) -> p b n", b=NB), i3,
                                          negm[:, :].rearrange("p (b o) -> p b o", o=1).to_broadcast([P, NB, P]), ALU.mult).then_inc(e["diag"], 1)
                        dve.wait_ge(e["pv"], past(nq * (hh + 1)))
                        if mode == "diff":
                            continue
                        ob = bank[5 + par]
                        dve.wait_ge(e["ylo"], past(hh))
                        if mode == "swa":
                            dve.wait_ge(e["es"], past(hh + 1))
                            dve.tensor_tensor(zt(31)[o, :], ob[o, :], extra[o, :], ALU.add).then_inc(e["rd"], 1)
                            dve.wait_ge(e["rd"], past(2 * hh + 1))
                            dve.reciprocal(rec[r, :], zt(31)[o, :]).then_inc(e["rd"], 1)
                            dve.wait_ge(e["rd"], past(2 * hh + 2))
                        else:
                            dve.reciprocal(rec[r, :], ob[o, :]).then_inc(e["rd"], 1)
                            dve.wait_ge(e["rd"], past(hh + 1))
                        dve.tensor_tensor(ytile[r, :], ob[r, :], rec[r, :], ALU.mult).then_inc(e["y"], 1)
                        dve.wait_ge(e["y"], past(hh + 1))
                        dve.wait_ge(e["yhi"], past(hh + 1))
                        dve.tensor_tensor(ylo[r, bass.ds(pp * S, S)], ytile[r, :], yhi[r, bass.ds(pp * S, S)], ALU.subtract).then_inc(e["ylo"], 1)
                    if mode == "diff":
                        c = 4 * pp
                        dve.wait_ge(e["ylo"], past(pp))
                        dve.reciprocal(rec, bank[2]).then_inc(e["rd"], 1)
                        dve.reciprocal(zt(31), bank[7]).then_inc(e["rd"], 1)
                        dve.wait_ge(e["rd"], past(c + 1))
                        dve.tensor_tensor(rec, bank[5], rec, ALU.mult).then_inc(e["rd"], 1)
                        dve.wait_ge(e["rd"], past(c + 2))
                        dve.scalar_tensor_tensor(zt(31), bank[6], lamv, zt(31), ALU.mult, ALU.mult).then_inc(e["rd"], 1)
                        dve.wait_ge(e["rd"], past(c + 4))
                        dve.tensor_tensor(zt(32), rec, zt(31), ALU.subtract).then_inc(e["y"], 1)
                        dve.wait_ge(e["nr"], past(pp + 1))
                        dve.scalar_tensor_tensor(ytile[:, :], zt(32), subg, zt(35), ALU.mult, ALU.mult).then_inc(e["yt"], 1)
                        dve.wait_ge(e["yt"], past(pp + 1))
                        dve.wait_ge(e["yhi"], past(pp + 1))
                        dve.tensor_tensor(ylo[:, bass.ds(pp * S, S)], ytile[:, :], yhi[:, bass.ds(pp * S, S)], ALU.subtract).then_inc(e["ylo"], 1)

                with dve.Fori(0, lay["loops"]) as j:
                    for s in range(lay["sub"]):
                        pair(j, s)

            for kind, st in steps:
                if kind == "bar":
                    bar()
                elif kind == "norm":
                    norm(*st)
                elif kind == "gemm":
                    gemm_units(st)
                elif kind == "lru":
                    lru()
                elif kind == "stick":
                    stick()
                else:
                    attn(**st)
            for n in range(2 * NB):
                dve.wait_ge(s_xt, DC + n + 1)
                dve.tensor_copy(zt(n), bank[n % 2]).then_inc(s_xc, 1)


_INS = [
    "x", "c", "ada_w", "ada_b", "norm_mix_g", "norm_ffn_g", "ev_w_in", "ev_conv_w", "ev_conv_b", "ev_wa", "ev_ba",
    "ev_wx", "ev_bx", "ev_lam", "ev_qn_g", "ev_kn_g", "ev_w_out", "od_w_in", "od_qn_g", "od_kn_g", "od_sinks",
    "od_w_out", "ffn_w_gate", "ffn_w_up", "ffn_conv_w", "ffn_conv_b", "ffn_w_down", "a_norm_2", "a_w_qkv_2",
    "a_q_gain_2", "a_k_gain_2", "a_lam_q1_2", "a_lam_k1_2", "a_lam_q2_2", "a_lam_k2_2", "a_sub_gain_2",
    "a_w_o_2", "kv_norm_2", "kv_w_2", "kv_k_gain_2", "b_norm_2", "b_w_q_2", "b_q_gain_2", "b_w_o_2", "m_norm_2",
    "m_w_up_2", "m_w_down_2",
]


def kernel(**inputs):
    import concourse.bacc as _bacc
    from concourse.bass_utils import run_bass_kernel_spmd as _run

    nc = _bacc.Bacc("TRN2", target_bir_lowering=False, num_devices=1)
    arrays, aps = {}, {}
    given = {n: np.ascontiguousarray(inputs[n]) for n in _INS}
    given.update(constants())
    for name, v in given.items():
        arrays[f"in_{name}"] = v
        aps[name] = nc.dram_tensor(f"in_{name}", v.shape, mybir.dt.from_np(v.dtype), kind="ExternalInput").ap()
    out = nc.dram_tensor("out_x", (1, S, D), F32, kind="ExternalOutput").ap()
    program(nc, aps, out)
    r = _run(nc, [arrays], core_ids=[0])
    return r.results[0]["out_x"]
```

```python
from contextlib import ExitStack
import math

import numpy as np

import concourse.bass as bass
from concourse import mybir

F32 = mybir.dt.float32
F32R = mybir.dt.float32r
BF16 = mybir.dt.bfloat16
ALU = mybir.AluOpType
ACT = mybir.ActivationFunctionType
AX = mybir.AxisListType

P = 128
S = 512
D = 1024
DC = D // P
DH = 64
NB = S // P
FF = 2816
FC = FF // P
PARTS = ((0, 8), (8, 8), (16, 6))
FF2 = 4096
LW = 512
LC = LW // P
EPS = 1e-6
NEG = -1e30
LAM_INIT = 0.8 - 0.6 * math.exp(-0.3 * 0)
GROUPS = 3
EXP_AND_LN = 6
CR = 16
DIL = (1, 4, 16)

M_PS, M_C1, M_PE, M_C, M_4, M_16, T_C, T_PS, T_PE, T_B, T_S = range(11)
N_MASK = 11


def constants():
    i = np.arange(P)[:, None]
    j = np.arange(P)[None, :]
    d = i - j
    allowed = [
        j > i, d >= 0, j >= i, d >= 0, d % 4 == 0, d % 16 == 0,
        d <= 0, i > j, i >= j,
        (d % 4 == 0) & (d <= 0), i < j,
    ]
    masks = np.stack([np.where(a, 0.0, NEG) for a in allowed], 1).astype(np.float32)
    inv = (1.0 / (np.float32(10000.0) ** (np.arange(0, DH, 2, dtype=np.float32) / np.float32(DH)))).astype(np.float32)
    ang = np.arange(S, dtype=np.float32)[None, :] * inv[:, None]
    cos = np.tile(np.cos(ang), (4, 1)).astype(np.float32)
    sin = np.tile(np.sin(ang), (4, 1)).astype(np.float32)
    heads = (i // DH == j // DH).astype(np.float32)
    rot = np.zeros((P, P), np.float32)
    for m in range(P):
        if m % DH < DH // 2:
            rot[m + DH // 2, m] = -1.0
        else:
            rot[m - DH // 2, m] = 1.0
    square = np.concatenate([
        np.eye(P, dtype=np.float32), np.ones((P, P), np.float32), heads, rot,
        np.where(i >= j, -1.0, 0.0).astype(np.float32), -np.ones((P, P), np.float32),
        cos, sin], 1)
    return {"masks": masks.reshape(P, N_MASK * P), "square": np.ascontiguousarray(square)}


class Params:

    def __init__(self):
        self.rows, self.at = 0, {}

    def add(self, name, n):
        self.at[name] = self.rows
        self.rows += n


def param_table():
    t = Params()
    for name, n in [("ada_b", 96), ("c", 8), ("norm_mix_g", 16), ("ev_ba", 4), ("ev_bx", 4),
                    ("norm_ffn_g", 16), ("a_norm", 8), ("kv_norm", 8), ("b_norm", 8), ("m_norm", 16),
                    ("ev_conv_w", 16), ("ev_conv_b", 4), ("ev_lam", 4), ("a_sub_gain", 1),
                    ("gains", 12), ("pad", 31),
                    ("ffn_conv_w", 132), ("ffn_conv_b", 44)]:
        t.add(name, n)
    return t


PT = param_table()
PT_TILES = -(-PT.rows // P)
GAINS = ["ev_qn_g", "ev_kn_g", "od_qn_g", "od_kn_g", "a_q_gain_2", "a_k_gain_2",
         "kv_k_gain_2", None, None, "b_q_gain_2", None, None]
G_EVQ, G_EVK, G_ODQ, G_ODK, G_AQ, G_AK, G_KV, G_B = 0, 1, 2, 3, 4, 5, 6, 9


class Stage:
    unit = 0
    seen = {}

    def __init__(self, kind, n, kc, weights, rhs, gain=0, dest=0, rope=False, perm=0, gate=None, source="", layer=0, first=0):
        self.kind, self.n, self.kc, self.weights, self.rhs = kind, n, kc, weights, rhs
        self.gain, self.dest, self.rope, self.perm, self.gate = gain, dest, rope, perm, gate
        self.source, self.layer, self.first = source, layer, first
        self.next_kc = None
        self.base = Stage.unit
        Stage.unit += n
        self.kbase = Stage.seen.get(kind, 0)
        Stage.seen[kind] = self.kbase + n
        self.rbase = Stage.seen.get("rope", 0)
        if rope:
            Stage.seen["rope"] = self.rbase + n


def program(nc, a, out):
    Stage.unit, Stage.seen = 0, {}
    ctx = ExitStack()

    def sb(name, shape, dt=F32, where=ctx):
        return where.enter_context(nc.sbuf_tensor(name, shape, dt))

    def sem(name):
        return ctx.enter_context(nc.semaphore(name))

    def past(n):
        return n + CR

    with ctx:
        raw = [sb(f"w_raw{j}", [P, DC * P]) for j in range(2)]
        whi = [sb(f"w_hi{j}", [P, DC * P], F32R) for j in range(2)]
        wlo = [sb(f"w_lo{j}", [P, DC * P], F32R) for j in range(2)]
        xT = sb("xT", [P, DC * S])
        yhi = sb("y_hi", [P, DC * S], F32R)
        ylo = sb("y_lo", [P, DC * S], F32R)
        sq9 = sb("squares", [P, 6 * P + 2 * S])
        ident, ones, blk64, rotm, ntri, nones = (sq9[:, k * P:(k + 1) * P] for k in range(6))
        cosT, sinT = sq9[:, 6 * P:6 * P + S], sq9[:, 6 * P + S:6 * P + 2 * S]
        maskb = sb("mask_b", [P, N_MASK * P], BF16)
        identb = sb("ident_b", [P, P], BF16)
        onesr = sb("ones_r", [P, P], F32R)
        PV = sb("params", [P, PT_TILES * P])
        MOD = sb("mods", [P, 96])
        NA = sb("norm_scale", [P, 4 * DC])
        small = sb("small", [P, 64])
        lamv = small[:, 0:1]
        m2 = sb("block_max", [P, 4 * GROUPS])
        negm = sb("neg_max", [P, NB])
        c8 = small[:, 4:8]
        sinkb = sb("sink_b", [P, 16])
        subg = small[:, 8:9]

        def mask(m):
            return maskb[:, m * P:(m + 1) * P]

        def masks_to(end, n):
            return maskb[:, (end - n) * P:end * P]

        def col(name, k=0, n=1):
            at = PT.at[name]
            return PV[:, at + k:at + k + n] if isinstance(k, int) else PV[:, bass.ds(k + at, n)]

        def gain(k):
            return PV[:, PT.at["gains"] + k:PT.at["gains"] + k + 1]

        u1 = ExitStack()
        with u1:
            hhi = sb("h_hi", [P, DC * S], F32R, u1)
            hlo = sb("h_lo", [P, DC * S], F32R, u1)
        u2 = ExitStack()
        with u2:
            qs_hi = sb("q_hi", [P, GROUPS * S], F32R, u2)
            qs_lo = sb("q_lo", [P, GROUPS * S], F32R, u2)
            ks_hi = sb("k_hi", [P, GROUPS * S], F32R, u2)
            ks_lo = sb("k_lo", [P, GROUPS * S], F32R, u2)
            diag = sb("diag", [P, 2 * S], F32R, u2)
            ytile = sb("y_tile", [P, S], F32, u2)
            extra = sb("extra", [P, S], F32, u2)
        sb("h_space", [P, 2 * DC * S])
        TMP = sb("tmp", [P, 8 * S])
        tmp = [TMP[:, j * S:(j + 1) * S] for j in range(8)]
        pad = sb("pad", [P, S + 3])
        z1 = ExitStack()
        with z1:
            Z = sb("Z", [P, 36 * S], F32, z1)
        z2 = ExitStack()
        with z2:
            mhi = sb("mid_hi", [P, DC * S], F32R, z2)
            mlo = sb("mid_lo", [P, DC * S], F32R, z2)
        sb("z_space", [P, 36 * S])

        PS = ctx.enter_context(nc.psum_tensor("banks", [P, 8 * S], F32))
        bank = [PS[:, j * S:(j + 1) * S] for j in range(8)]
        G = bank[0:2]

        def zt(k, n=1):
            return Z[:, k * S:(k + n) * S] if isinstance(k, int) else Z[:, bass.ds(k * S, n * S)]

        def ch(t, k, w=S):
            return t[:, k * w:(k + 1) * w] if isinstance(k, int) else t[:, bass.ds(k * w, w)]

        w_raw = [sem("w_raw0"), sem("w_raw1")]
        s_whi, s_wlo = sem("w_hi_ready"), sem("w_lo_ready")
        gemm = sem("gemm_done")
        evac = [sem("evac0"), sem("evac1")]
        bar_pe, bar_act, bar_dve = sem("bar_pe"), sem("bar_act"), sem("bar_dve")
        s_const, s_par, s_x, s_ini, s_out = (sem(n) for n in ("consts", "par", "x_in", "ini", "out_done"))
        s_pt, s_ptc, s_zero = sem("par_t"), sem("par_c"), sem("zeroed")
        s_adaw = [sem(f"ada_w{j}") for j in range(4)]
        s_ada = sem("ada_done")
        s_xt, s_xc = sem("x_t"), sem("x_c")
        n_sq, n_ss, n_ln, n_rstd, n_t, n_hi, n_lo = (sem("n_" + n) for n in ("sq", "ss", "ln", "rstd", "t", "hi", "lo"))
        h_sq, h_ss, h_ln, h_rstd, h_qn, h_rot, h_a, h_b, h_out = (
            sem("h_" + n) for n in ("sq", "ss", "ln", "rstd", "qn", "rot", "a", "b", "out"))
        v_tp, v_out = sem("v_tp"), sem("v_out")
        cv = sem("conv_step")
        f_cv, f_silu, f_hi, f_lo = (sem("f_" + n) for n in ("conv", "silu", "hi", "lo"))
        r_r, r_hi, r_lo = (sem("r_" + n) for n in ("relu", "hi", "lo"))
        l_g, l_a, l_d, l_y = sem("l_gate"), sem("l_act"), sem("l_dve"), sem("l_yhi")
        dv, av = sem("dve_chain"), sem("act_chain")

        W = {n: a[n] for n in a}

        def cols_of(w, k0, kc, first, per):
            def view(i):
                n0 = first + per * i
                c = w[k0:k0 + kc * P, n0:n0 + P] if isinstance(n0, int) else w[k0:k0 + kc * P, bass.ds(n0, P)]
                return c.rearrange("(c p) n -> p c n", p=P)
            return view

        steps = []

        def gemm_stage(kind, n, kc, w, rhs, k0=0, first=0, gain=0, dest=0, rope=False, perm=0, gate=None, source=""):
            st = Stage(kind, n, kc, [cols_of(w, k0, kc, first, 2 * P), cols_of(w, k0, kc, first + P, 2 * P)], rhs,
                       gain=gain, dest=dest, rope=rope, perm=perm, gate=gate, source=source)
            steps.append(("gemm", st))

        norms = [0]

        def norm_step(scale, shift):
            steps.append(("bar", None))
            steps.append(("norm", (norms[0], scale, shift)))
            norms[0] += 1

        def ffn(layer):
            norm_step(lambda c: NA[:, (2 * layer + 1) * DC + c:(2 * layer + 1) * DC + c + 1],
                      lambda c: MOD[:, layer * 48 + 24 + c:layer * 48 + 25 + c])
            wg, wu, wd = (a[n][layer] for n in ("ffn_w_gate", "ffn_w_up", "ffn_w_down"))
            for c0, n in PARTS:
                st = Stage("ffn", 2 * n, DC, [cols_of(wg, 0, DC, c0 * P, P), cols_of(wu, 0, DC, c0 * P, P)],
                           "h", layer=layer, first=c0)
                steps.append(("gemm", st))
                gemm_stage("down", DC, n, wd, "mid", k0=c0 * P, gate=layer * 48 + 40, source="f")

        def mlp(layer):
            norm_step(lambda c: col("m_norm", layer * DC + c), None)
            for part in range(FF2 // D):
                gemm_stage("relu", DC, DC, a["m_w_up_2"][layer], "h", first=part * D)
                gemm_stage("down", DC, DC, a["m_w_down_2"][layer], "mid", k0=part * D, gate=None, source="r")

        norm_step(lambda c: NA[:, c:c + 1], lambda c: MOD[:, c:c + 1])
        ev = a["ev_w_in"][0]
        gemm_stage("conv", 4, DC, ev, "h", first=0)
        gemm_stage("gelu", 4, DC, ev, "h", first=LW)
        steps.append(("bar", None))
        steps.append(("lru", None))
        steps.append(("bar", None))
        gemm_stage("head", 4, DC, ev, "h", first=2 * LW, gain=G_EVQ, dest=24, rope=False)
        gemm_stage("head", 4, DC, ev, "h", first=3 * LW, gain=G_EVK, dest=28, rope=False)
        gemm_stage("v", 4, DC, ev, "h", first=4 * LW, dest=32, perm=0)
        steps += [("bar", None), ("stick", None), ("bar", None)]
        gemm_stage("down", 8, DC, a["ev_w_out"][0], "y", gate=16)
        ffn(0)
        norm_step(lambda c: NA[:, 2 * DC + c:2 * DC + c + 1], lambda c: MOD[:, 48 + c:49 + c])
        od = a["od_w_in"][0]
        gemm_stage("head", 8, DC, od, "h", first=0, gain=G_ODQ, dest=0, rope=False)
        gemm_stage("head", 2, DC, od, "h", first=D, gain=G_ODK, dest=8, rope=False)
        gemm_stage("v", 2, DC, od, "h", first=D + 256, dest=10, perm=0)
        steps += [("bar", None), ("attn", dict(mode="swa", base=0)), ("bar", None)]
        gemm_stage("down", 8, DC, a["od_w_out"][0], "y", gate=48 + 16)
        ffn(1)
        norm_step(lambda c: col("a_norm", c), None)
        qkv = a["a_w_qkv_2"][0]
        gemm_stage("head", 8, DC, qkv, "h", first=0, gain=G_AQ, dest=0, rope=True)
        gemm_stage("head", 8, DC, qkv, "h", first=D, gain=G_AK, dest=8, rope=True)
        gemm_stage("v", 8, DC, qkv, "h", first=2 * D, dest=16, perm=0)
        steps += [("bar", None), ("attn", dict(mode="diff", base=0)), ("bar", None)]
        gemm_stage("down", 8, DC, a["a_w_o_2"][0], "y", gate=None)
        mlp(0)
        for half in range(2):
            norm_step(lambda c: col("kv_norm", c), None)
            for g in range(GROUPS):
                gemm_stage("head", 4, DC, a["kv_w_2"], "h", first=g * D + half * 512, gain=G_KV + g, dest=12 + 4 * g, rope=True)
            for g in range(GROUPS):
                gemm_stage("v", 4, DC, a["kv_w_2"], "h", first=3 * D + g * D + half * 512, dest=24 + 4 * g, perm=g)
            norm_step(lambda c: col("b_norm", c), None)
            for g in range(GROUPS):
                gemm_stage("head", 4, DC, a["b_w_q_2"][0], "h", first=g * D + half * 512, gain=G_B + g, dest=4 * g, rope=True)
            steps += [("bar", None), ("attn", dict(mode="dil", base=4 * half))]
        steps.append(("bar", None))
        gemm_stage("down", 8, DC, a["b_w_o_2"][0], "y", gate=None)
        mlp(1)
        steps.append(("bar", None))

        stages = [st for k, st in steps if k == "gemm"]
        for s0, s1 in zip(stages, stages[1:] + [None]):
            s0.next_kc = s1.kc if s1 else None
            assert s0.base % 2 == 0

        at = {}
        for mode in ("swa", "diff", "dil"):
            at[mode] = {e: sem(f"{mode}_{e}") for e in
                        ("qhi", "qlo", "v", "mx", "red", "negm", "diag", "st", "p", "pv", "rd", "y", "yhi", "ylo", "e", "es", "nrm", "nss", "nl", "nr", "yd", "yt")}
        stk = {e: sem(f"stick_{e}") for e in ("hi", "lo", "v", "z", "ab", "ex", "ln", "sp", "rev", "w", "pv", "yhi", "ylo")}

        def par_rows():
            src = {"c": a["c"], "a_sub_gain": a["a_sub_gain_2"], "ev_conv_w": a["ev_conv_w"][0].rearrange("j n -> (j n)"),
                   "ffn_conv_w": a["ffn_conv_w"].rearrange("l j n -> (l j n)")}
            for name in PT.at:
                if name in ("gains", "pad"):
                    continue
                v = src.get(name)
                if v is None:
                    v = a[name] if name in a else a[name + "_2"]
                if len(v.shape) == 2:
                    v = v.rearrange("l n -> (l n)")
                v = v.rearrange("(r n) -> r n", n=P)
                r0, n, done = PT.at[name], v.shape[0], 0
                while done < n:
                    t, o = divmod(r0 + done, P)
                    m = min(n - done, P - o)
                    yield tmp[t][o:o + m, 0:P], v[done:done + m, :]
                    done += m
            for k, name in enumerate(GAINS):
                if name is None:
                    continue
                v = a[name][0] if len(a[name].shape) == 3 else a[name]
                t, o = divmod(PT.at["gains"] + k, P)
                for s in range(2):
                    yield tmp[t][o:o + v.shape[0], DH * s:DH * (s + 1)], v
            for k, (q, kk) in enumerate((("a_lam_q1_2", "a_lam_k1_2"), ("a_lam_q2_2", "a_lam_k2_2"))):
                yield tmp[4 + k][:, 0:DH], a[q].to_broadcast([P, DH])
                yield tmp[4 + k][:, DH:2 * DH], a[kk].to_broadcast([P, DH])
            yield sinkb[:, :], a["od_sinks"].to_broadcast([P, 16])

        par_loads = list(par_rows())
        N_PAR = len(par_loads)
        dv2, s_kdup, s_vd = sem("dve_start"), sem("k_dup"), sem("v_rows")
        eps = small[:, 60:61]

        def starts(eng, owned):
            for s in owned:
                eng.sem_inc(s, CR)

        def quads(mode, g):
            if mode == "diff":
                return [[(0, S - kt * P, kt, kt * P, [(0, T_C)])] for kt in range(NB)]
            if g == 0:
                prev = T_PS if mode == "swa" else T_PE
                r = [(0, 256, 0, 0, [(0, T_C), (P, prev)]), (256, 256, 1, P, [(0, T_C), (P, prev)])]
                r2 = [(0, 256, 2, 2 * P, [(0, T_C), (P, prev)]), (256, P, 3, 3 * P, [(0, T_C)])]
                return [r, r2]
            m = T_C if g == 1 else T_B
            return [[(c * P, P, c, c, [(0, m)]) for c in range(NB)]]

        def perm(g, c, n, first):
            def view(t, off):
                if g == 0:
                    return t[:, off + first:off + first + n]
                v = t[:, off:off + S]
                return v.rearrange("p (l s) -> p s l", s=4)[:, c, :]
            return view

        def quad_list(mode):
            gs = range(GROUPS) if mode == "dil" else [0]
            return [(g, q) for g in gs for q in quads(mode, g)]

        def layout(mode):
            if mode == "swa":
                return dict(loops=4, sub=2, ng=1, q=lambda j, s, g: 2 * j + s, k=None, nq=2)
            if mode == "diff":
                return dict(loops=4, sub=2, ng=1, q=lambda j, s, g: 2 * j + s, k=lambda j, s, g: 8 + 2 * j + s, nq=4)
            return dict(loops=4, sub=1, ng=3, q=lambda j, s, g: 4 * g + j, k=lambda j, s, g: 12 + 4 * g + j, nq=4)

        def fills(mode):
            if mode == "swa":
                return [(0, [(0, 0, 0), (256, 0, 1)]), (1, [(0, 0, 2), (256, 0, 3)])]
            if mode == "diff":
                return [(0, [(0, 0, 3)]), (1, [(0, 0, 2), (3 * P, 0, 0)]), (0, [(0, 0, 1)])]
            return [(0, [(0, 0, 0), (256, 0, 1)]), (1, [(0, 0, 2), (256, 0, 3)]),
                    (2, [(0, 1, 3)]), (7, [(0, 1, 2), (3 * P, 1, 0)]), (0, [(0, 1, 1), (256, 2, 1)]),
                    (1, [(0, 2, 3)]), (2, [(0, 2, 2), (3 * P, 2, 0)])]

        def fill_width(mode, g, b):
            return P * (b + 1 if mode == "diff" or g > 0 else min(b + 1, 2))

        def run_heads(eng, lay, slot):
            def body(j, first, last):
                seq = [(j, s, par) for s in range(lay["sub"]) for par in range(2)]
                for i, cur in enumerate(seq):
                    past_heads = [] if first else [(j - 1, lay["sub"] - 1, par) for par in range(2)]
                    past_heads = ([None, None] + past_heads + seq[:i])[-2:]
                    nxt = seq[i + 1] if i + 1 < len(seq) else (None if last else (j + 1, 0, 0))
                    slot(past_heads[1], cur, nxt, last, past_heads[0])

            n = lay["loops"]
            body(0, True, False)
            with eng.Fori(1, n - 1) as j:
                body(j, False, False)
            body(n - 1, False, True)

        def pair_after(lay, j, s, last):
            if s + 1 < lay["sub"]:
                return j, s + 1
            return None if last else (j + 1, 0)

        KDUP = 14
        ST = bank[3:5]

        VW = 3 * DH

        def room(mode):
            if mode == "dil":
                return TMP[:, 0:12 * VW], [TMP[:, 12 * VW + j * S:12 * VW + (j + 1) * S] for j in range(2)], TMP[:, 12 * VW + 2 * S:12 * VW + 3 * S]
            return zt(24, 2) if mode == "diff" else Z[:, 24 * S:24 * S + NB * VW], [zt(26 + j) for j in range(4)], zt(30)

        block = ctx.enter_context(nc.Block())

        @block.sync
        def _(sp):
            sp.dma_start(sq9[:, :], a["square"]).then_inc(s_const, 16)
            sp.dma_start(Z[:, 0:N_MASK * P], a["masks"]).then_inc(s_const, 16)
            sp.wait_ge(s_zero, 1)
            for w, name in enumerate(("ev_wa", "ev_wx")):
                for b in range(2):
                    tiles = Z[64 * b:64 * b + 64, 32 * S:34 * S].rearrange("p (t w n) -> p t w n", w=2, n=P)
                    sp.dma_start(tiles[:, :, w, 64 * b:64 * b + 64],
                                 a[name][0].rearrange("(t b) k j -> b k t j", b=2)[b]).then_inc(s_const, 16)
            sp.dma_start(zt(6, 8).rearrange("p (b d) -> p b d", b=NB),
                         a["x"][0].rearrange("(b p) d -> p b d", p=P)).then_inc(s_x, 16)
            slab = DC * 2 * P
            for n in range(48):
                if n >= 4:
                    sp.wait_ge(s_ada, n - 3)
                layer, c0 = divmod(n * 2 * P, 6 * D)
                sp.dma_start(Z[:, 16 * S + (n % 4) * slab:16 * S + (n % 4 + 1) * slab].rearrange("p (c n) -> p c n", c=DC),
                             a["ada_w"][layer][:, c0:c0 + 2 * P].rearrange("(c p) n -> p c n", p=P)).then_inc(s_adaw[n % 4], 16)

            def load(st, i, j):
                u = st.base + j + 2 * i
                half = st.base // 2 + i
                sp.wait_ge(s_wlo, past(u - 1))
                sp.dma_start(raw[j][:, 0:st.kc * P].rearrange("p (c n) -> p c n", n=P), st.weights[j](i)).then_inc(w_raw[j], 16)

            for st in stages:
                lo = 0
                if st.base == 0:
                    load(st, 0, 0)
                    load(st, 0, 1)
                    lo = 1
                if st.n // 2 - lo <= 1:
                    for i in range(lo, st.n // 2):
                        load(st, i, 0)
                        load(st, i, 1)
                else:
                    with sp.Fori(lo, st.n // 2) as i:
                        load(st, i, 0)
                        load(st, i, 1)
            for t in range(NB):
                for hh in range(2):
                    sp.wait_ge(s_xc, DC + 2 * t + hh + 1)
                    sp.dma_start(out[0, t * P:(t + 1) * P, hh * S:(hh + 1) * S], zt(2 * t + hh)).then_inc(s_out, 16)
            sp.wait_ge(s_out, 16 * 2 * NB)

        @block.gpsimd
        def _(pool):
            starts(pool, [s_wlo])

            def split(st, i, j):
                u = st.base + j + 2 * i
                pool.wait_ge(s_whi, past(u + 1))
                n = st.kc * P
                pool.tensor_tensor(wlo[j][:, 0:n], raw[j][:, 0:n], whi[j][:, 0:n], ALU.subtract).then_inc(s_wlo, 1)

            for st in stages:
                if st.n <= 2:
                    split(st, 0, 0)
                    split(st, 0, 1)
                else:
                    with pool.Fori(0, st.n // 2) as i:
                        split(st, i, 0)
                        split(st, i, 1)

        def run_units(eng, st, do):
            b, n = st.base, st.n

            def unit(i, par):
                return 2 * i + par, par, 2 * i + (b + par), i + b // 2

            do(unit(0, 0), None)
            if n > 4:
                with eng.Fori(0, (n - 2) // 2) as i:
                    do(unit(i, 1), unit(i, 0))
                    do(unit(i + 1, 0), unit(i, 1))
            elif n == 4:
                do(unit(0, 1), unit(0, 0))
                do(unit(1, 0), unit(0, 1))
            do(unit(n // 2 - 1, 1), unit(n // 2 - 1, 0))

        @block.tensor
        def _(pe):
            starts(pe, [at[m][e] for m in at for e in ("mx", "st", "pv", "e", "nss")] + [stk[e] for e in ("z", "rev", "pv")]
                   + [h_ss, h_rot, v_tp, n_ss, gemm])
            nbar = [0]
            pending = [None]

            def bar():
                flush()
                nbar[0] += 1
                pe.drain().then_inc(bar_pe, 1)
                pe.wait_ge(bar_act, nbar[0])
                pe.wait_ge(bar_dve, nbar[0])

            def flush():
                if pending[0]:
                    pending[0]("a")
                    pending[0]("b")
                pending[0] = None

            def post(st, l, par, u, half):
                k = st.kbase + l
                kr = st.rbase + l

                def head(part):
                    if part == "a":
                        pe.wait_ge(h_sq, past(k + 1))
                        pe.wait_ge(h_ln, past(k))
                        pe.matmul(bank[2], blk64, tmp[0], start=True, stop=True).then_inc(h_ss, 1)
                    elif st.rope:
                        pe.wait_ge(h_qn, past(k + 1))
                        pe.wait_ge(h_out, past(kr))
                        pe.matmul(bank[3], rotm, tmp[2], start=True, stop=True).then_inc(h_rot, 1)

                def vpost(part):
                    if part == "a":
                        pe.wait_ge(evac[par], past(half + 1))
                        pe.wait_ge(v_out, past(k))
                        for c in range(NB):
                            view = perm(st.perm, c, P, c * P)(tmp[4], 0)
                            mm = pe.transpose(bank[4][:, c * P:(c + 1) * P], view, ident)
                        mm.then_inc(v_tp, 1)

                return {"head": head, "v": vpost}.get(st.kind, lambda part: None)

            def gemm_units(st):
                hi, lo = {"h": (hhi, hlo), "y": (yhi, ylo), "mid": (mhi, mlo)}[st.rhs]
                def do(this, before):
                    l, par, u, half = this
                    follow = post(st, *before) if before else pending[0]
                    g = G[par]
                    first = isinstance(l, int) and l == 0
                    pe.wait_ge(evac[par], past(half))
                    pe.wait_ge(s_whi, past(u + 1))
                    for k in range(st.kc):
                        ready(st, first, "hi", k)
                        pe.matmul(g, whi[par][:, k * P:(k + 1) * P], hi[:, k * S:(k + 1) * S], start=(k == 0), stop=False)
                    if follow:
                        follow("a")
                    for k in range(st.kc):
                        ready(st, first, "lo", k)
                        pe.matmul(g, whi[par][:, k * P:(k + 1) * P], lo[:, k * S:(k + 1) * S], start=False, stop=False)
                    pe.wait_ge(s_wlo, past(u + 1))
                    for k in range(st.kc):
                        mm = pe.matmul(g, wlo[par][:, k * P:(k + 1) * P], hi[:, k * S:(k + 1) * S], start=False, stop=(k == st.kc - 1))
                    mm.then_inc(gemm, 1)
                    if follow:
                        follow("b")
                    if isinstance(l, int) and l == st.n - 1:
                        pending[0] = post(st, *this)

                run_units(pe, st, do)

            def ready(st, first, part, k):
                if not first:
                    return
                high = part == "hi"
                if st.rhs == "h":
                    pe.wait_ge(n_hi if high else n_lo, past((norm_seen[0] - 1) * DC + k + 1))
                elif st.source == "f":
                    pe.wait_ge(f_hi if high else f_lo, past(mid_base["f"] + k + 1))
                elif st.source == "r":
                    pe.wait_ge(r_hi if high else r_lo, past(mid_base["r"] + k + 1))

            norm_seen = [0]
            mid_base = {"f": 0, "r": 0}

            def norm(ni, scale, shift):
                norm_seen[0] = ni + 1
                for c in range(DC):
                    pe.wait_ge(n_sq, past(DC * ni + c + 1))
                    pe.matmul(bank[2], ones, tmp[c % 2], start=(c == 0), stop=(c == DC - 1)).then_inc(n_ss, 1)

            pe.wait_ge(s_const, 96)
            pe.wait_ge(s_par, 16 * N_PAR)
            for t in range(PT_TILES):
                pe.transpose(bank[t][:, 0:P], tmp[t][:, 0:P], ident).then_inc(s_pt, 1)
            pe.wait_ge(s_x, 16)
            for c in range(DC):
                if c >= 2:
                    pe.wait_ge(s_xc, c - 1)
                for b in range(NB):
                    mm = pe.transpose(bank[5 + c % 2][:, b * P:(b + 1) * P], Z[:, 6 * S + b * D + c * P:6 * S + b * D + (c + 1) * P], ident)
                mm.then_inc(s_xt, 1)
            pe.wait_ge(s_ini, 1)
            for n in range(48):
                pe.wait_ge(s_adaw[n % 4], 16 * (n // 4 + 1))
                base = 16 * S + (n % 4) * DC * 2 * P
                for j in range(2):
                    for k in range(DC):
                        mm = pe.matmul(bank[7][:, 2 * n + j:2 * n + j + 1], Z[:, base + k * 256 + j * P:base + k * 256 + (j + 1) * P],
                                       small[:, 16 + k:17 + k], start=(k == 0), stop=(k == DC - 1))
                mm.then_inc(s_ada, 1)

            def lru():
                for t in range(LC):
                    for w in range(2):
                        wt = Z[:, 32 * S + (2 * t + w) * P:32 * S + (2 * t + w + 1) * P]
                        mm = pe.matmul(bank[4 * w + t], wt, zt(t), start=True, stop=True)
                        mm.then_inc(l_g, 1)

            def stick():
                e = stk
                def head(i, par):
                    h = 2 * i + par
                    r = slice(64 * par, 64 * par + 64)
                    for kt in range(NB - 1, -1, -1):
                        n = S - kt * P
                        z = bank[kt]
                        pe.wait_ge(e["w"], past(4 * h - kt))
                        ks = slice(kt * P, (kt + 1) * P)
                        pe.matmul(z[:, 0:n], ks_hi[r, ks], qs_hi[r, kt * P:S], start=True, stop=False)
                        pe.matmul(z[:, 0:n], ks_hi[r, ks], qs_lo[r, kt * P:S], start=False, stop=False)
                        pe.matmul(z[:, 0:P], identb[:, :], mask(T_S), start=False, stop=False, skip_group_check=True)
                        pe.matmul(z[:, 0:n], ks_lo[r, ks], qs_hi[r, kt * P:S], start=False, stop=True).then_inc(e["z"], 1)
                    for kt in range(NB - 1, -1, -1):
                        n = S - kt * P
                        z = bank[kt]
                        pe.wait_ge(e["sp"], past(4 * h + NB - kt))
                        for k2 in range(NB - 1, kt, -1):
                            o = (k2 - kt) * P
                            pe.matmul(z[:, o:n], nones, zt(16 + k2)[:, 0:S - k2 * P], start=False, stop=False, skip_group_check=True)
                        pe.matmul(z[:, 0:n], ntri, zt(16 + kt)[:, 0:n], start=False, stop=True, skip_group_check=True).then_inc(e["rev"], 1)
                    pe.wait_ge(e["v"], past(i + 1))
                    pe.wait_ge(e["ylo"], past(h))
                    for kt in range(NB - 1, -1, -1):
                        n = S - kt * P
                        pe.wait_ge(e["w"], past(4 * h + NB - kt))
                        mm = pe.matmul(bank[4][r, kt * P:S], zt(8)[:, kt * P + 64 * par:kt * P + 64 * par + 64],
                                       zt(9 + kt)[:, 0:n], start=(kt == NB - 1), stop=(kt == 0), skip_group_check=True)
                    mm.then_inc(e["pv"], 1)

                with pe.Fori(0, 4) as i:
                    pe.wait_ge(e["lo"], past(2 * i + 2))
                    for par in range(2):
                        head(i, par)

            def attn(mode, base):
                e, lay, ql, fl = at[mode], layout(mode), quad_list(mode), fills(mode)
                nq, ng, nf = len(ql), lay["ng"], len(fl)
                vals, probs, _ = room(mode)
                np_ = min(nq, len(probs))

                def pair_of(head):
                    j, s, par = head
                    return base + lay["sub"] * j + s, s, par

                def maxima(head):
                    pp, s, par = pair_of(head)
                    hh = 2 * pp + par
                    r = slice(64 * par, 64 * par + 64)
                    seen = 0
                    for f, (bk, regions) in enumerate(fl):
                        before = [i for i in range(f) if fl[i][0] == bk]
                        after = [i for i in range(nf) if fl[i][0] == bk]
                        pe.wait_ge(e["red"], past(nf * hh + before[-1] + 1 if before else nf * (hh - 1) + after[-1] + 1))
                        if mode == "diff" and bk == 1:
                            pe.wait_ge(e["nl"], past(pp - 2 + par))
                        for c0, g, b in regions:
                            if par == 0 and seen <= g:
                                seen = g + 1
                                pe.wait_ge(e["qhi"], past(2 * ng * pp + 2 * seen))
                            n = fill_width(mode, g, b)
                            at_ = (s if ng == 1 else g) * S
                            q = qs_hi[r, at_ + b * P:at_ + (b + 1) * P]
                            k = ks_hi[r, at_ + (b + 1) * P - n:at_ + (b + 1) * P]
                            m = bank[bk]
                            if mode == "diff":
                                if b:
                                    pe.matmul(m[:, c0:c0 + n - P], q, k[:, 0:n - P], start=True, stop=True)
                                pe.matmul(m[:, c0 + n - P:c0 + n], identb[:, :], mask(M_C), start=True, stop=False)
                                mm = pe.matmul(m[:, c0 + n - P:c0 + n], q, k[:, n - P:n], start=False, stop=True)
                                continue
                            if g == 0:
                                pe.matmul(m[:, c0:c0 + n], identb[:, :], masks_to((M_C1 if mode == "swa" else M_C) + 1, n // P), start=True, stop=False)
                            else:
                                off = mask(M_4 if g == 1 else M_16).rearrange("p (o n) -> p o n", o=1).to_broadcast([P, b + 1, P])
                                pe.matmul(m[:, c0:c0 + n].rearrange("p (o n) -> p o n", o=b + 1), identb[:, :], off, start=True, stop=False)
                                pe.matmul(m[:, c0 + n - P:c0 + n], identb[:, :], mask(M_C), start=False, stop=False, skip_group_check=True)
                            mm = pe.matmul(m[:, c0:c0 + n], q, k, start=False, stop=True)
                        mm.then_inc(e["mx"], 1)

                def scores(head, q):
                    pp, s, par = pair_of(head)
                    hh = 2 * pp + par
                    r = slice(64 * par, 64 * par + 64)
                    g, regions = ql[q]
                    at_ = (s if ng == 1 else g) * S
                    t = ST[q % 2]
                    pe.wait_ge(e["p"], past(nq * hh + q - 1))
                    for c0, n, c, first, masks in regions:
                        kv = perm(g, c, P, c * P)
                        qv = perm(g, c, n, first)
                        o = t[:, c0:c0 + n]
                        kh, kl = kv(ks_hi[r, :], at_), kv(ks_lo[r, :], at_)
                        qh, ql_ = qv(qs_hi[r, :], at_), qv(qs_lo[r, :], at_)
                        pe.matmul(o, kh, qh, start=True, stop=False)
                        pe.matmul(o, kh, ql_, start=False, stop=False)
                        pe.matmul(o, kl, qh, start=False, stop=False)
                        for off, m in masks:
                            pe.matmul(t[:, c0 + off:c0 + off + P], identb[:, :], mask(m), start=False, stop=False, skip_group_check=True)
                        mm = pe.matmul(o, onesr[:, :], qv(diag[:, :], par * S), start=False, stop=True)
                    mm.then_inc(e["st"], 1)

                def values(head, q):
                    pp, s, par = pair_of(head)
                    hh = 2 * pp + par
                    g, regions = ql[q]
                    pe.wait_ge(e["p"], past(nq * hh + q + 1))
                    if q == 0:
                        pe.wait_ge(e["v"], past(head[0] + 1 if mode == "swa" else pp + 1))
                        pe.wait_ge(e["y"], past(hh - 1))
                    pb = probs[q % np_]
                    for ri, (c0, n, c, first, _) in enumerate(regions):
                        rhs = pb[:, c0:c0 + n]
                        st_, sp_ = (q == 0 and ri == 0), (q == nq - 1 and ri == len(regions) - 1)
                        if mode == "diff":
                            vt = vals[:, s * S + c * P:s * S + (c + 1) * P]
                            pe.matmul(bank[5 + par][:, first:first + n], vt, rhs, start=st_, stop=sp_, skip_group_check=True)
                            mm = pe.matmul(bank[(2, 7)[par]][:, first:first + n], ones, rhs, start=st_, stop=sp_, skip_group_check=True)
                        else:
                            vt = vals[:, (g * NB + c) * VW + 64 * par:(g * NB + c) * VW + 64 * par + P]
                            o = perm(g, c, n, first)(bank[5 + par], 0)
                            mm = pe.matmul(o, vt, rhs, start=st_, stop=sp_, skip_group_check=True)
                    mm.then_inc(e["pv"], 1)

                def mean_square(pp):
                    pe.wait_ge(e["nrm"], past(pp + 1))
                    pe.matmul(bank[1], ones, zt(33), start=True, stop=True).then_inc(e["nss"], 1)

                def slot(prev, cur, nxt, last, prev2):
                    pp, s, par = pair_of(cur)
                    hh = 2 * pp + par
                    if par == 0:
                        pe.wait_ge(e["qlo"], past((2 * ng) * (pp + 1)))
                    pe.wait_ge(e["diag"], past(hh + 1))
                    if mode == "swa":
                        pe.wait_ge(e["es"], past(hh))
                        pe.matmul(bank[7], onesr[:, :], diag[:, par * S:(par + 1) * S], start=True, stop=True).then_inc(e["e"], 1)
                    late = mode == "dil" and nxt and nxt[2] == 0
                    for q in range(nq):
                        scores(cur, q)
                        if nxt and q == (nq - 1 if late else 0):
                            maxima(nxt)
                        if q == 0 and prev:
                            values(prev, nq - 1)
                        if q:
                            values(cur, q - 1)
                        if mode == "diff" and par and q == 2 and prev2:
                            pe.wait_ge(e["red"], past(nf * (hh + 1) + (2 if nxt else 0)))
                            mean_square(pp - 1)

                maxima((0, 0, 0))
                run_heads(pe, lay, slot)
                end = (lay["loops"] - 1, lay["sub"] - 1, 1)
                values(end, nq - 1)
                if mode == "diff":
                    mean_square(base + lay["loops"] * lay["sub"] - 1)

            for kind, st in steps:
                if kind == "bar":
                    bar()
                elif kind == "norm":
                    norm(*st)
                elif kind == "gemm":
                    gemm_units(st)
                    if st.kind == "down" and st.rhs == "mid":
                        mid_base[st.source] += st.kc
                elif kind == "lru":
                    lru()
                elif kind == "stick":
                    stick()
                else:
                    attn(**st)
            for t in range(NB):
                for hh in range(2):
                    n = 2 * t + hh
                    if n >= 2:
                        pe.wait_ge(s_xc, DC + n - 1)
                    for c in range(4):
                        cc = 4 * hh + c
                        mm = pe.transpose(bank[n % 2][:, c * P:(c + 1) * P], xT[:, cc * S + t * P:cc * S + (t + 1) * P], ident)
                    mm.then_inc(s_xt, 1)


        @block.scalar
        def _(act):
            starts(act, [at[m][e] for m in at for e in ("qhi", "p", "yhi", "es", "nrm", "nl", "nr")]
                   + [stk[e] for e in ("hi", "ab", "ex", "ln", "w", "yhi")]
                   + [h_sq, h_ln, h_rstd, f_silu, f_hi, r_r, r_hi, n_sq, n_ln, n_rstd, n_hi, s_whi])
            nbar, pending, other_tables = [0], [None], [False]

            def exp_and_ln():
                act.add_instruction(mybir.InstLoadActFuncSet(
                    name=nc.get_next_instruction_name(), act_func_set_id=EXP_AND_LN, ins=[], outs=[],
                    engine=mybir.EngineType.Activation))
                other_tables[0] = False

            def bar():
                if pending[0]:
                    pending[0]()
                pending[0] = None
                if other_tables[0]:
                    exp_and_ln()
                nbar[0] += 1
                act.drain().then_inc(bar_act, 1)
                act.wait_ge(bar_pe, nbar[0])
                act.wait_ge(bar_dve, nbar[0])

            act.wait_ge(s_zero, 1)
            for dst, src in par_loads:
                act.dma_start(dst, src).then_inc(s_par, 16)
            act.wait_ge(s_ptc, PT_TILES)
            act.activation(small[:, 16:24], col("c", 0, 8), ACT.Silu).then_inc(s_ini, 1)
            exp_and_ln()
            act.activation(small[:, 24:28], col("ev_lam", 0, 4), ACT.Abs).then_inc(av, 1)
            act.wait_ge(av, 1)
            act.activation(small[:, 28:32], small[:, 24:28], ACT.Exp, scale=-1.0).then_inc(av, 1)
            act.wait_ge(dv, 1)
            act.activation(small[:, 36:40], small[:, 32:36], ACT.Ln).then_inc(av, 1)
            act.wait_ge(dv, 3)
            act.activation(small[:, 42:44], small[:, 40:42], ACT.Exp).then_inc(av, 1)

            def high(kc, par, u, half):
                act.wait_ge(w_raw[par], 16 * (half + 1))
                act.wait_ge(gemm, past(u - 1))
                act.activation(whi[par][:, 0:kc * P], raw[par][:, 0:kc * P], ACT.Copy).then_inc(s_whi, 1)

            def post(st, l, par, u, half):
                t = half - st.base // 2
                k = st.kbase + l

                def head():
                    act.wait_ge(gemm, past(u + 1))
                    act.wait_ge(h_ss, past(k))
                    act.activation(tmp[0], G[par], ACT.Square).then_inc(h_sq, 1)
                    act.wait_ge(h_qn, past(k))
                    act.activation(tmp[1], G[par], ACT.Copy).then_inc(evac[par], 1)
                    act.wait_ge(h_ss, past(k + 1))
                    act.wait_ge(h_rstd, past(k))
                    act.activation(tmp[3], bank[2], ACT.Ln, bias=eps, scale=1.0 / DH).then_inc(h_ln, 1)
                    act.wait_ge(h_ln, past(k + 1))
                    act.activation(tmp[6], tmp[3], ACT.Exp, scale=-0.5).then_inc(h_rstd, 1)

                def v():
                    act.wait_ge(gemm, past(u + 1))
                    act.wait_ge(v_tp, past(k))
                    act.activation(tmp[4], G[par], ACT.Copy).then_inc(evac[par], 1)

                def gelu():
                    act.wait_ge(gemm, past(u + 1))
                    act.activation(zt(4 + l), G[par], ACT.Gelu_apprx_tanh).then_inc(evac[par], 1)

                def ffn():
                    kf = st.kbase // 2 + t
                    if par == 0:
                        act.wait_ge(f_cv, past(3 * (kf + 1)))
                        act.wait_ge(evac[1], past(half))
                        act.activation(tmp[1], tmp[0], ACT.Silu).then_inc(f_silu, 1)
                    else:
                        act.wait_ge(evac[1], past(half + 1))
                        act.activation(ch(mhi, t), tmp[2], ACT.Copy).then_inc(f_hi, 1)

                def relu():
                    act.wait_ge(gemm, past(u + 1))
                    act.activation(tmp[0], G[par], ACT.Relu).then_inc(r_r, 1)
                    act.wait_ge(evac[par], past(half + 1))
                    act.activation(ch(mhi, l), tmp[1], ACT.Copy).then_inc(r_hi, 1)

                return {"head": head, "v": v, "gelu": gelu, "ffn": ffn, "relu": relu}.get(st.kind, lambda: None)

            def gemm_units(st):
                def do(this, before):
                    l, par, u, half = this
                    last = isinstance(l, int) and l == st.n - 1
                    kc = st.next_kc if last else st.kc
                    if kc:
                        high(kc, 1 - par, u + 1, half + par)
                    follow = post(st, *before) if before else pending[0]
                    if follow:
                        follow()
                    if last:
                        pending[0] = post(st, *this)

                run_units(act, st, do)

            def norm(ni, scale, shift):
                for c in range(DC):
                    act.wait_ge(n_ss, past(DC * ni + c - 1))
                    act.activation(tmp[c % 2], ch(xT, c), ACT.Square).then_inc(n_sq, 1)
                act.wait_ge(n_ss, past(DC * (ni + 1)))
                act.activation(tmp[2], bank[2], ACT.Ln, bias=eps, scale=1.0 / D).then_inc(n_ln, 1)
                act.wait_ge(n_ln, past(ni + 1))
                act.activation(tmp[3], tmp[2], ACT.Exp, scale=-0.5).then_inc(n_rstd, 1)
                for c in range(DC):
                    act.wait_ge(n_t, past(DC * ni + c + 1))
                    if shift:
                        act.activation(ch(hhi, c), tmp[4 + c % 2], ACT.Identity, bias=shift(c)).then_inc(n_hi, 1)
                    else:
                        act.activation(ch(hhi, c), tmp[4 + c % 2], ACT.Copy).then_inc(n_hi, 1)

            def lru():
                for t in range(LC):
                    act.wait_ge(l_g, 2 * t + 1)
                    act.activation(zt(8 + t), bank[t], ACT.Sigmoid, bias=col("ev_ba", t)).then_inc(l_a, 1)
                    act.wait_ge(l_g, 2 * t + 2)
                    act.activation(zt(12 + t), bank[4 + t], ACT.Sigmoid, bias=col("ev_bx", t)).then_inc(l_a, 1)
                act.wait_ge(l_a, 8)
                for t in range(LC):
                    act.activation(zt(16 + t), zt(8 + t), ACT.Tanh, scale=c8[:, t:t + 1]).then_inc(l_a, 1)
                for t in range(LC):
                    act.activation(zt(8 + t), zt(8 + t), ACT.Exp, scale=c8[:, t:t + 1]).then_inc(l_a, 1)
                act.wait_ge(l_d, 3)
                act.activation(zt(20, 4), zt(20, 4), ACT.Sqrt).then_inc(l_a, 1)
                act.wait_ge(l_d, 10)
                act.activation(yhi[:, 0:LC * S], zt(16, 4), ACT.Copy).then_inc(l_y, 1)

            def stick():
                e = stk

                def pair(i):
                    act.wait_ge(e["z"], past(8 * i))
                    act.activation(qs_hi[:, 0:S], zt(i + 24), ACT.Copy).then_inc(e["hi"], 1)
                    act.activation(ks_hi[:, 0:S], zt(i + 28), ACT.Copy).then_inc(e["hi"], 1)
                    for par in range(2):
                        h = 2 * i + par
                        for kt in range(NB - 1, -1, -1):
                            n = S - kt * P
                            c = 4 * h + NB - kt
                            act.wait_ge(e["z"], past(c))
                            act.wait_ge(e["ex"], past(c - 1))
                            act.activation(zt(13)[:, 0:n], bank[kt][:, 0:n], ACT.Abs).then_inc(e["ab"], 1)
                            act.wait_ge(e["ab"], past(c))
                            act.wait_ge(e["ln"], past(c - 1))
                            act.activation(zt(14)[:, 0:n], zt(13)[:, 0:n], ACT.Exp, scale=-1.0).then_inc(e["ex"], 1)
                            act.wait_ge(e["ex"], past(c))
                            act.wait_ge(e["sp"], past(c - 4))
                            act.activation(zt(20 + kt)[:, 0:n], zt(14)[:, 0:n], ACT.Ln, bias=1.0).then_inc(e["ln"], 1)
                        for kt in range(NB - 1, -1, -1):
                            n = S - kt * P
                            act.wait_ge(e["rev"], past(4 * h + NB - kt))
                            act.wait_ge(e["pv"], past(h))
                            act.activation(zt(9 + kt)[:, 0:n], bank[kt][:, 0:n], ACT.Exp).then_inc(e["w"], 1)
                        r = slice(64 * par, 64 * par + 64)
                        act.wait_ge(e["pv"], past(h + 1))
                        act.activation(yhi[r, bass.ds((i + 4) * S, S)], bank[4][r, :], ACT.Copy).then_inc(e["yhi"], 1)

                with act.Fori(0, 4) as i:
                    pair(i)

            def attn(mode, base):
                e, lay, ql = at[mode], layout(mode), quad_list(mode)
                nq, ng = len(ql), lay["ng"]
                vals, probs, rec = room(mode)
                np_ = min(nq, len(probs))
                last_quad = [max(q for q in range(nq) if ql[q][0] == g) for g in range(ng)]

                def high_parts(j, s, g):
                    pp = base + lay["sub"] * j + s
                    if ng == 1:
                        act.wait_ge(e["st"], past(nq * 2 * (pp - 1)))
                    else:
                        act.wait_ge(e["st"], past(nq * (2 * pp - 1) + last_quad[g] + 1))
                    k = s if ng == 1 else g
                    act.activation(ch(qs_hi, k), zt(lay["q"](j, s, g)), ACT.Copy).then_inc(e["qhi"], 1)
                    src = zt(KDUP + j) if mode == "swa" else zt(lay["k"](j, s, g))
                    act.activation(ch(ks_hi, k), src, ACT.Copy).then_inc(e["qhi"], 1)

                def y_high(head):
                    j, s, par = head
                    pp = base + lay["sub"] * j + s
                    r = slice(64 * par, 64 * par + 64)
                    act.wait_ge(e["y"], past(2 * pp + par + 1))
                    y = yhi[r, pp * S:(pp + 1) * S] if isinstance(pp, int) else yhi[r, bass.ds(pp * S, S)]
                    act.activation(y, ytile[r, :], ACT.Copy).then_inc(e["yhi"], 1)

                def sub_square(pp):
                    act.wait_ge(e["yd"], past(pp + 1))
                    act.wait_ge(e["nss"], past(pp))
                    act.activation(zt(33), zt(32), ACT.Square).then_inc(e["nrm"], 1)

                def sub_scale(pp):
                    act.wait_ge(e["nss"], past(pp + 1))
                    act.wait_ge(e["nr"], past(pp))
                    act.activation(zt(34), bank[1], ACT.Ln, bias=eps, scale=1.0 / P).then_inc(e["nl"], 1)
                    act.wait_ge(e["nl"], past(pp + 1))
                    act.wait_ge(e["yt"], past(pp))
                    act.activation(zt(35), zt(34), ACT.Exp, scale=-0.5).then_inc(e["nr"], 1)

                def sub_high(pp):
                    act.wait_ge(e["yt"], past(pp + 1))
                    act.activation(ch(yhi, pp), ytile[:, :], ACT.Copy).then_inc(e["yhi"], 1)

                def slot(prev, cur, nxt, last, prev2):
                    j, s, par = cur
                    pp = base + lay["sub"] * j + s
                    hh = 2 * pp + par
                    o = slice(64 - 64 * par, 128 - 64 * par)
                    after = pair_after(lay, j, s, last)
                    if ng == 1 and par == 0 and after:
                        high_parts(*after, 0)
                    if mode == "swa":
                        act.wait_ge(e["e"], past(hh + 1))
                        act.wait_ge(e["rd"], past(2 * (hh - 1)))
                        act.activation(extra[o, :], bank[7][o, :], ACT.Exp, bias=sinkb[o, bass.ds(4 * j + 2 * s + par, 1)]).then_inc(e["es"], 1)
                    for q, (g, regions) in enumerate(ql):
                        n = sum(x[1] for x in regions)
                        act.wait_ge(e["st"], past(nq * hh + q + 1))
                        act.wait_ge(e["pv"], past(nq * hh + q + 1 - np_))
                        act.activation(probs[q % np_][:, 0:n], ST[q % 2][:, 0:n], ACT.Exp).then_inc(e["p"], 1)
                        if mode == "diff" and q == 1 and par == 0 and prev2 and not (isinstance(pp, int) and pp < base + 2):
                            sub_high(pp - 2)
                        if mode == "dil" and nxt and nxt[2] == 0 and q >= 1:
                            high_parts(nxt[0], 0, g)
                    if mode != "diff":
                        if prev:
                            y_high(prev)
                    elif prev2:
                        if par == 0:
                            sub_square(pp - 1)
                        else:
                            sub_scale(pp - 1)

                if mode == "swa":
                    act.wait_ge(s_kdup, 1)
                for g in range(ng):
                    high_parts(0, 0, g)
                run_heads(act, lay, slot)
                if mode == "diff":
                    pp = base + lay["loops"] * lay["sub"] - 1
                    sub_high(pp - 1)
                    sub_square(pp)
                    sub_scale(pp)
                    sub_high(pp)
                else:
                    y_high((lay["loops"] - 1, lay["sub"] - 1, 1))

            high(DC, 0, 0, 0)
            for kind, st in steps:
                if kind == "bar":
                    bar()
                elif kind == "norm":
                    norm(*st)
                elif kind == "gemm":
                    gemm_units(st)
                    other_tables[0] = other_tables[0] or st.kind == "ffn"
                elif kind == "lru":
                    lru()
                    other_tables[0] = True
                elif kind == "stick":
                    stick()
                else:
                    attn(**st)

        @block.vector
        def _(dve):
            starts(dve, [at[m][e] for m in at for e in ("qlo", "v", "red", "negm", "diag", "rd", "y", "ylo", "yd", "yt")]
                   + [stk[e] for e in ("lo", "v", "sp", "ylo")]
                   + [*evac, n_t, n_lo, h_qn, h_a, h_b, h_out, v_out, cv, f_cv, f_lo, r_lo])
            nbar, pending = [0], [None]

            def bar():
                if pending[0]:
                    pending[0]()
                pending[0] = None
                nbar[0] += 1
                dve.drain().then_inc(bar_dve, 1)
                dve.wait_ge(bar_pe, nbar[0])
                dve.wait_ge(bar_act, nbar[0])

            steps_done = [0]

            def link(ins):
                steps_done[0] += 1
                ins.then_inc(dv2, 1)
                dve.wait_ge(dv2, steps_done[0])

            dve.memset(eps, EPS)
            dve.memset(TMP[:, :], 0.0)
            dve.memset(pad[:, 0:3], 0.0)
            dve.memset(Z[:, 32 * S:34 * S], 0.0).then_inc(s_zero, 1)
            dve.wait_ge(s_const, 96)
            dve.tensor_copy(maskb[:, :], Z[:, 0:N_MASK * P])
            dve.tensor_copy(identb[:, :], ident)
            dve.tensor_copy(onesr[:, :], ones)
            for t in range(PT_TILES):
                dve.wait_ge(s_pt, t + 1)
                dve.tensor_copy(PV[:, t * P:(t + 1) * P], bank[t][:, 0:P]).then_inc(s_ptc, 1)
            dve.wait_ge(s_ptc, PT_TILES)
            for k in (G_EVQ, G_ODQ, G_AQ, G_B, G_B + 1, G_B + 2):
                dve.tensor_scalar(gain(k), gain(k), DH ** -0.5, None, ALU.mult)
            dve.tensor_scalar(subg, col("a_sub_gain"), 1.0 - LAM_INIT, None, ALU.mult)
            dve.wait_ge(av, 2)
            e1, w1, l1 = small[:, 28:32], small[:, 32:36], small[:, 36:40]
            dve.tensor_scalar(w1, e1, 1.0, None, ALU.add).then_inc(dv, 1)
            for k in range(2):
                dve.tensor_tensor_reduce(out=tmp[4 + k][:, 128:192], in0=tmp[4 + k][:, 0:64],
                                         in1=tmp[4 + k][:, 64:128], scale=1.0, scalar=0.0, op0=ALU.mult, op1=ALU.add,
                                         accum_out=small[:, 40 + k:41 + k]).then_inc(dv, 1)
            dve.wait_ge(dv, 1)
            link(dve.scalar_tensor_tensor(small[:, 44:48], w1, -1.0, e1, ALU.add, ALU.subtract))
            link(dve.reciprocal(small[:, 48:52], w1))
            link(dve.tensor_tensor(small[:, 44:48], small[:, 44:48], small[:, 48:52], ALU.mult))
            dve.wait_ge(av, 3)
            link(dve.tensor_tensor(small[:, 44:48], l1, small[:, 44:48], ALU.subtract))
            link(dve.tensor_scalar(small[:, 48:52], col("ev_lam", 0, 4), -1.0, 0.0, ALU.mult, ALU.max))
            link(dve.tensor_tensor(small[:, 44:48], small[:, 44:48], small[:, 48:52], ALU.add))
            link(dve.tensor_scalar(c8, small[:, 44:48], -8.0, None, ALU.mult))
            dve.wait_ge(av, 4)
            link(dve.scalar_tensor_tensor(lamv, small[:, 42:43], LAM_INIT, small[:, 43:44], ALU.add, ALU.subtract))
            for c in range(DC):
                dve.wait_ge(s_xt, c + 1)
                dve.tensor_copy(ch(xT, c), bank[5 + c % 2]).then_inc(s_xc, 1)
            dve.wait_ge(s_ada, 48)
            link(dve.tensor_tensor(MOD[:, :], bank[7][:, 0:96], col("ada_b", 0, 96), ALU.add))
            for layer in range(2):
                for w, name in enumerate(("norm_mix_g", "norm_ffn_g")):
                    o = (2 * layer + w) * DC
                    m = layer * 48 + 8 + 24 * w
                    link(dve.scalar_tensor_tensor(NA[:, o:o + DC], MOD[:, m:m + DC], 1.0, col(name, layer * DC, DC), ALU.add, ALU.mult))

            def post(st, l, par, u, half):
                t = half - st.base // 2
                k = st.kbase + l
                kr = st.rbase + l

                def conv():
                    dve.wait_ge(gemm, past(u + 1))
                    dve.wait_ge(cv, past(4 * l))
                    dve.tensor_copy(pad[:, 3:3 + S], G[par]).then_inc(evac[par], 1)
                    dve.wait_ge(evac[par], past(half + 1))
                    dve.tensor_scalar(zt(l), pad[:, 3:3 + S], col("ev_conv_w", 12 + l), col("ev_conv_b", l), ALU.mult, ALU.add).then_inc(cv, 1)
                    for j in range(1, 4):
                        dve.wait_ge(cv, past(4 * l + j))
                        dve.scalar_tensor_tensor(zt(l), pad[:, 3 - j:3 - j + S], col("ev_conv_w", 4 * (3 - j) + l), zt(l), ALU.mult, ALU.add).then_inc(cv, 1)

                def head():
                    dve.wait_ge(h_rstd, past(k + 1))
                    dve.wait_ge(evac[par], past(half + 1))
                    dest = zt(st.dest + l)
                    if st.rope:
                        dve.wait_ge(h_out, past(kr))
                    dve.scalar_tensor_tensor(tmp[2] if st.rope else dest, tmp[1], gain(st.gain), tmp[6], ALU.mult, ALU.mult).then_inc(h_qn, 1)
                    if st.rope:
                        dve.wait_ge(h_qn, past(k + 1))
                        dve.tensor_tensor(tmp[7], tmp[2], cosT, ALU.mult).then_inc(h_a, 1)
                        dve.wait_ge(h_rot, past(kr + 1))
                        dve.tensor_tensor(tmp[5], bank[3], sinT, ALU.mult).then_inc(h_b, 1)
                        dve.wait_ge(h_a, past(kr + 1))
                        dve.wait_ge(h_b, past(kr + 1))
                        dve.tensor_tensor(dest, tmp[7], tmp[5], ALU.add).then_inc(h_out, 1)

                def v():
                    dve.wait_ge(v_tp, past(k + 1))
                    dve.tensor_scalar(zt(st.dest + l), bank[4], 1.0, None, ALU.mult).then_inc(v_out, 1)

                def ffn():
                    kf = st.kbase // 2 + t
                    if par == 0:
                        o = st.first
                        w = lambda j: col("ffn_conv_w", t + ((st.layer * 3 + j) * FC + o))
                        dve.wait_ge(gemm, past(u + 1))
                        dve.wait_ge(f_cv, past(3 * kf))
                        dve.tensor_copy(pad[:, 3:3 + S], G[0]).then_inc(evac[0], 1)
                        dve.wait_ge(evac[0], past(half + 1))
                        dve.wait_ge(f_silu, past(kf))
                        dve.tensor_scalar(tmp[0], pad[:, 3:3 + S], w(2), col("ffn_conv_b", t + (st.layer * FC + o)), ALU.mult, ALU.add).then_inc(f_cv, 1)
                        for j in range(1, 3):
                            dve.wait_ge(f_cv, past(3 * kf + j))
                            dve.scalar_tensor_tensor(tmp[0], pad[:, 3 - j:3 - j + S], w(2 - j), tmp[0], ALU.mult, ALU.add).then_inc(f_cv, 1)
                    else:
                        dve.wait_ge(gemm, past(u + 1))
                        dve.wait_ge(f_silu, past(kf + 1))
                        dve.wait_ge(f_lo, past(kf))
                        dve.tensor_tensor(tmp[2], G[1], tmp[1], ALU.mult).then_inc(evac[1], 1)
                        dve.wait_ge(f_hi, past(kf + 1))
                        dve.tensor_tensor(ch(mlo, t), tmp[2], ch(mhi, t), ALU.subtract).then_inc(f_lo, 1)

                def relu():
                    dve.wait_ge(r_r, past(k + 1))
                    dve.wait_ge(r_lo, past(k))
                    dve.scalar_tensor_tensor(tmp[1], G[par], 0.0, tmp[0], ALU.max, ALU.mult).then_inc(evac[par], 1)
                    dve.wait_ge(r_hi, past(k + 1))
                    dve.tensor_tensor(ch(mlo, l), tmp[1], ch(mhi, l), ALU.subtract).then_inc(r_lo, 1)

                def down():
                    dve.wait_ge(gemm, past(u + 1))
                    dve.wait_ge(evac[par], past(half))
                    x = ch(xT, l)
                    if st.gate is None:
                        dve.tensor_tensor(x, G[par], x, ALU.add).then_inc(evac[par], 1)
                    else:
                        g = MOD[:, st.gate + l:st.gate + l + 1] if isinstance(l, int) else MOD[:, bass.ds(l + st.gate, 1)]
                        dve.scalar_tensor_tensor(x, G[par], g, x, ALU.mult, ALU.add).then_inc(evac[par], 1)

                return {"conv": conv, "head": head, "v": v, "ffn": ffn, "relu": relu, "down": down}.get(st.kind, lambda: None)

            def gemm_units(st):
                def do(this, before):
                    follow = post(st, *before) if before else pending[0]
                    if follow:
                        follow()
                    if isinstance(this[0], int) and this[0] == st.n - 1:
                        pending[0] = post(st, *this)

                run_units(dve, st, do)

            def norm(ni, scale, shift):
                dve.wait_ge(n_rstd, past(ni + 1))

                def low(c):
                    dve.wait_ge(n_hi, past(DC * ni + c + 1))
                    if shift:
                        dve.scalar_tensor_tensor(ch(hlo, c), tmp[4 + c % 2], shift(c), ch(hhi, c), ALU.add, ALU.subtract).then_inc(n_lo, 1)
                    else:
                        dve.tensor_tensor(ch(hlo, c), tmp[4 + c % 2], ch(hhi, c), ALU.subtract).then_inc(n_lo, 1)

                for c in range(DC):
                    dve.wait_ge(n_lo, past(DC * ni + c - 1))
                    dve.scalar_tensor_tensor(tmp[4 + c % 2], ch(xT, c), scale(c), tmp[3], ALU.mult, ALU.mult).then_inc(n_t, 1)
                    if c:
                        low(c - 1)
                low(DC - 1)

            def lru():
                A, I, T, U = zt(8, 4), zt(12, 4), zt(16, 4), zt(20, 4)
                dve.wait_ge(l_a, 16)
                dve.tensor_scalar(U, T, -1.0, 1.0, ALU.mult, ALU.add).then_inc(l_d, 1)
                dve.wait_ge(l_d, 1)
                dve.reciprocal(U, U).then_inc(l_d, 1)
                dve.wait_ge(l_d, 2)
                dve.scalar_tensor_tensor(U, T, -2.0, U, ALU.mult, ALU.mult).then_inc(l_d, 1)
                dve.tensor_tensor(I, I, zt(0, 4), ALU.mult).then_inc(l_d, 1)
                dve.wait_ge(l_a, 17)
                dve.wait_ge(l_d, 4)
                dve.tensor_tensor(U, U, I, ALU.mult).then_inc(l_d, 1)
                dve.wait_ge(l_d, 5)
                for t in range(LC):
                    dve.tensor_tensor_scan(zt(16 + t), zt(8 + t), zt(20 + t), 0.0, ALU.mult, ALU.add).then_inc(l_d, 1)
                dve.wait_ge(l_d, 9)
                dve.tensor_tensor(T, T, zt(4, 4), ALU.mult).then_inc(l_d, 1)
                dve.wait_ge(l_d, 10)
                dve.wait_ge(l_y, 1)
                dve.tensor_tensor(ylo[:, 0:LC * S], T, yhi[:, 0:LC * S], ALU.subtract)

            def stick():
                e = stk
                with dve.Fori(0, 4) as i:
                    dve.wait_ge(e["hi"], past(2 * i + 1))
                    dve.tensor_tensor(qs_lo[:, 0:S], zt(i + 24), qs_hi[:, 0:S], ALU.subtract).then_inc(e["lo"], 1)
                    dve.wait_ge(e["hi"], past(2 * i + 2))
                    dve.tensor_tensor(ks_lo[:, 0:S], zt(i + 28), ks_hi[:, 0:S], ALU.subtract).then_inc(e["lo"], 1)
                    dve.wait_ge(e["pv"], past(2 * i))
                    dve.tensor_scalar(zt(8), zt(i + 32), 1.0, None, ALU.mult).then_inc(e["v"], 1)
                    for par in range(2):
                        h = 2 * i + par
                        for kt in range(NB - 1, -1, -1):
                            n = S - kt * P
                            dve.wait_ge(e["ln"], past(4 * h + NB - kt))
                            dve.wait_ge(e["rev"], past(4 * h))
                            dve.scalar_tensor_tensor(zt(16 + kt)[:, 0:n], bank[kt][:, 0:n], 0.0, zt(20 + kt)[:, 0:n], ALU.max, ALU.add).then_inc(e["sp"], 1)
                        r = slice(64 * par, 64 * par + 64)
                        dve.wait_ge(e["yhi"], past(h + 1))
                        dve.tensor_tensor(ylo[r, bass.ds((i + 4) * S, S)], bank[4][r, :], yhi[r, bass.ds((i + 4) * S, S)], ALU.subtract).then_inc(e["ylo"], 1)

            def attn(mode, base):
                e, lay, ql, fl = at[mode], layout(mode), quad_list(mode), fills(mode)
                nq, ng, nf = len(ql), lay["ng"], len(fl)
                vals, probs, rec = room(mode)
                i3 = ident.rearrange("p (o n) -> p o n", o=1).to_broadcast([P, NB, P])

                if mode == "swa":
                    for kv in range(4):
                        src = zt(8 + kv // 2)[64 * (kv % 2):64 * (kv % 2) + 64, :]
                        for o in range(2):
                            dve.tensor_copy(zt(KDUP + kv)[64 * o:64 * o + 64, :], src)
                        dve.tensor_copy(Z[:, 18 * S + kv * 256:18 * S + (kv + 1) * 256].rearrange("p (c d) -> p c d", d=DH),
                                        zt(10 + kv // 2).rearrange("p (c d) -> p c d", d=P)[:, :, 64 * (kv % 2):64 * (kv % 2) + 64]).then_inc(s_vd, 1)
                    dve.wait_ge(s_vd, 4)
                    dve.drain().then_inc(s_kdup, 1)
                    dve.wait_ge(s_kdup, 1)
                if mode != "diff":
                    n = ng * NB
                    v4 = vals.rearrange("p (c h d) -> p c h d", h=3, d=DH)
                    dve.memset(v4[:, :, 1, :], 1.0)

                def values(j, s):
                    pp = base + lay["sub"] * j + s
                    if mode == "diff":
                        dve.wait_ge(e["pv"], past(nq * 2 * (pp - 1)))
                        dve.tensor_scalar(vals[:, s * S:(s + 1) * S], zt(2 * j + (16 + s)), 1.0, None, ALU.mult).then_inc(e["v"], 1)
                        return
                    dve.wait_ge(e["pv"], past(nq * 2 * pp))
                    for g in range(ng):
                        for par in range(2):
                            if mode == "swa":
                                src = Z[:, bass.ds(18 * S + j * 256, 256)].rearrange("p (c d) -> p c d", d=DH)
                            else:
                                src = zt(24 + 4 * g + j).rearrange("p (c d) -> p c d", d=P)[:, :, 64 * par:64 * par + 64]
                            ins = dve.tensor_scalar(v4[:, g * NB:(g + 1) * NB, 2 * par, :], src, 1.0, None, ALU.mult)
                    ins.then_inc(e["v"], 1)

                def low_parts(j, s):
                    pp = base + lay["sub"] * j + s
                    for g in range(ng):
                        k = s if ng == 1 else g
                        dve.wait_ge(e["qhi"], past(2 * ng * pp + 2 * g + 1))
                        dve.tensor_tensor(ch(qs_lo, k), zt(lay["q"](j, s, g)), ch(qs_hi, k), ALU.subtract).then_inc(e["qlo"], 1)
                        dve.wait_ge(e["qhi"], past(2 * ng * pp + 2 * g + 2))
                        src = zt(KDUP + j) if mode == "swa" else zt(lay["k"](j, s, g))
                        dve.tensor_tensor(ch(ks_lo, k), src, ch(ks_hi, k), ALU.subtract).then_inc(e["qlo"], 1)

                def maxima(head):
                    j, s, par = head
                    hh = 2 * (base + lay["sub"] * j + s) + par
                    dve.wait_ge(e["negm"], past(hh))
                    for f, (bk, regions) in enumerate(fl):
                        dve.wait_ge(e["mx"], past(nf * hh + f + 1))
                        for c0, g, b in regions:
                            n = fill_width(mode, g, b)
                            ins = dve.tensor_reduce(m2[:, ng * b + g:ng * b + g + 1], bank[bk][:, c0:c0 + n], AX.X, ALU.max)
                        ins.then_inc(e["red"], 1)
                    dve.wait_ge(e["red"], past(nf * (hh + 1)))
                    dve.wait_ge(e["diag"], past(hh))
                    if mode == "dil":
                        dve.tensor_reduce(negm[:, :], m2[:, :].rearrange("p (b g) -> p b g", g=ng), AX.X, ALU.max, negate=True).then_inc(e["negm"], 1)
                    elif mode == "swa":
                        dve.tensor_scalar(negm[:, :], m2[:, 0:4], sinkb[:, bass.ds(4 * j + 2 * s + par, 1)], -1.0, ALU.max, ALU.mult).then_inc(e["negm"], 1)
                    else:
                        dve.tensor_scalar(negm[:, :], m2[:, 0:4], -1.0, None, ALU.mult).then_inc(e["negm"], 1)
                    dve.wait_ge(e["negm"], past(hh + 1))
                    dve.wait_ge(e["st"], past(nq * (hh - 1)))
                    dve.tensor_tensor(diag[:, par * S:(par + 1) * S].rearrange("p (b n) -> p b n", b=NB), i3,
                                      negm[:, :].rearrange("p (b o) -> p b o", o=1).to_broadcast([P, NB, P]), ALU.mult).then_inc(e["diag"], 1)

                def finish(head):
                    j, s, par = head
                    pp = base + lay["sub"] * j + s
                    hh = 2 * pp + par
                    r = slice(64 * par, 64 * par + 64)
                    o = slice(64 - 64 * par, 128 - 64 * par)
                    ob = bank[5 + par]
                    dve.wait_ge(e["pv"], past(nq * (hh + 1)))
                    if mode == "diff":
                        dve.wait_ge(e["y"], past(hh))
                        dve.reciprocal(rec, bank[(2, 7)[par]]).then_inc(e["rd"], 1)
                        dve.wait_ge(e["rd"], past(hh + 1))
                        if par == 0:
                            dve.wait_ge(e["yd"], past(pp))
                            dve.tensor_tensor(zt(31), ob, rec, ALU.mult).then_inc(e["y"], 1)
                        else:
                            dve.scalar_tensor_tensor(rec, ob, lamv, rec, ALU.mult, ALU.mult).then_inc(e["y"], 1)
                            dve.wait_ge(e["y"], past(hh + 1))
                            dve.wait_ge(e["yt"], past(pp))
                            dve.wait_ge(e["nrm"], past(pp))
                            dve.tensor_tensor(zt(32), zt(31), rec, ALU.subtract).then_inc(e["yd"], 1)
                            dve.wait_ge(e["yd"], past(pp + 1))
                        return
                    if mode == "swa":
                        dve.wait_ge(e["es"], past(hh + 1))
                        dve.tensor_tensor(zt(31)[o, :], ob[o, :], extra[o, :], ALU.add).then_inc(e["rd"], 1)
                        dve.wait_ge(e["rd"], past(2 * hh + 1))
                        dve.reciprocal(rec[r, :], zt(31)[o, :]).then_inc(e["rd"], 1)
                        dve.wait_ge(e["rd"], past(2 * hh + 2))
                    else:
                        dve.reciprocal(rec[r, :], ob[o, :]).then_inc(e["rd"], 1)
                        dve.wait_ge(e["rd"], past(hh + 1))
                    dve.wait_ge(e["ylo"], past(hh - 1))
                    dve.tensor_tensor(ytile[r, :], ob[r, :], rec[r, :], ALU.mult).then_inc(e["y"], 1)

                def y_low(head):
                    j, s, par = head
                    pp = base + lay["sub"] * j + s
                    r = slice(64 * par, 64 * par + 64)
                    dve.wait_ge(e["yhi"], past(2 * pp + par + 1))
                    if isinstance(pp, int):
                        c = slice(pp * S, (pp + 1) * S)
                    else:
                        c = bass.ds(pp * S, S)
                    dve.tensor_tensor(ylo[r, c], ytile[r, :], yhi[r, c], ALU.subtract).then_inc(e["ylo"], 1)

                def sub_norm(pp):
                    dve.wait_ge(e["nr"], past(pp + 1))
                    dve.wait_ge(e["ylo"], past(pp))
                    dve.scalar_tensor_tensor(ytile[:, :], zt(32), subg, zt(35), ALU.mult, ALU.mult).then_inc(e["yt"], 1)

                def sub_low(pp):
                    dve.wait_ge(e["yhi"], past(pp + 1))
                    dve.tensor_tensor(ch(ylo, pp), ytile[:, :], ch(yhi, pp), ALU.subtract).then_inc(e["ylo"], 1)

                def slot(prev, cur, nxt, last, prev2):
                    j, s, par = cur
                    pp = base + lay["sub"] * j + s
                    after = pair_after(lay, j, s, last)
                    if ng == 1 and par == 0 and after:
                        low_parts(*after)
                    if mode == "dil" and nxt and nxt[2] == 0:
                        low_parts(nxt[0], 0)
                    if nxt:
                        maxima(nxt)
                    if mode == "diff" and par == 0 and after:
                        values(*after)
                    if mode != "diff" and s == 0 and par == 0 and prev:
                        values(j, 0)
                    if prev:
                        finish(prev)
                    if mode != "diff":
                        if prev2:
                            y_low(prev2)
                    elif prev2:
                        if par:
                            sub_norm(pp - 1)
                        elif not (isinstance(pp, int) and pp < base + 2):
                            sub_low(pp - 2)

                low_parts(0, 0)
                values(0, 0)
                maxima((0, 0, 0))
                run_heads(dve, lay, slot)
                end = (lay["loops"] - 1, lay["sub"] - 1)
                finish((*end, 1))
                if mode == "diff":
                    pp = base + lay["loops"] * lay["sub"] - 1
                    sub_low(pp - 1)
                    sub_norm(pp)
                    sub_low(pp)
                else:
                    y_low((*end, 0))
                    y_low((*end, 1))

            for kind, st in steps:
                if kind == "bar":
                    bar()
                elif kind == "norm":
                    norm(*st)
                elif kind == "gemm":
                    gemm_units(st)
                elif kind == "lru":
                    lru()
                elif kind == "stick":
                    stick()
                else:
                    attn(**st)
            for n in range(2 * NB):
                dve.wait_ge(s_xt, DC + n + 1)
                dve.tensor_copy(zt(n), bank[n % 2]).then_inc(s_xc, 1)


_INS = [
    "x", "c", "ada_w", "ada_b", "norm_mix_g", "norm_ffn_g", "ev_w_in", "ev_conv_w", "ev_conv_b", "ev_wa", "ev_ba",
    "ev_wx", "ev_bx", "ev_lam", "ev_qn_g", "ev_kn_g", "ev_w_out", "od_w_in", "od_qn_g", "od_kn_g", "od_sinks",
    "od_w_out", "ffn_w_gate", "ffn_w_up", "ffn_conv_w", "ffn_conv_b", "ffn_w_down", "a_norm_2", "a_w_qkv_2",
    "a_q_gain_2", "a_k_gain_2", "a_lam_q1_2", "a_lam_k1_2", "a_lam_q2_2", "a_lam_k2_2", "a_sub_gain_2",
    "a_w_o_2", "kv_norm_2", "kv_w_2", "kv_k_gain_2", "b_norm_2", "b_w_q_2", "b_q_gain_2", "b_w_o_2", "m_norm_2",
    "m_w_up_2", "m_w_down_2",
]


def kernel(**inputs):
    import concourse.bacc as _bacc
    from concourse.bass_utils import run_bass_kernel_spmd as _run

    nc = _bacc.Bacc("TRN2", target_bir_lowering=False, num_devices=1)
    arrays, aps = {}, {}
    given = {n: np.ascontiguousarray(inputs[n]) for n in _INS}
    given.update(constants())
    for name, v in given.items():
        arrays[f"in_{name}"] = v
        aps[name] = nc.dram_tensor(f"in_{name}", v.shape, mybir.dt.from_np(v.dtype), kind="ExternalInput").ap()
    out = nc.dram_tensor("out_x", (1, S, D), F32, kind="ExternalOutput").ap()
    program(nc, aps, out)
    r = _run(nc, [arrays], core_ids=[0])
    return r.results[0]["out_x"]
```
